# Optimizing a Trainium2 kernel written in Bass

```python
import jax, jax.numpy as jnp
from jax import lax
import numpy as np

D_MODEL = 4096
BATCH = 1
SEQ = 256
DEPTH = 1

CHUNK = 64
WINDOW = 128
WIN_CHUNKS = WINDOW // CHUNK
ATTN_HEAD_DIM = 128
ATTN_Q_HEADS = D_MODEL // 256
ATTN_KV_HEADS = ATTN_Q_HEADS // 4
ATTN_WIDTH = ATTN_Q_HEADS * ATTN_HEAD_DIM
KV_WIDTH = ATTN_KV_HEADS * ATTN_HEAD_DIM
HGRN_HEADS = D_MODEL // 256
HGRN_EXPAND = 128
HGRN_HEAD_V = 128
HGRN_WIDTH = HGRN_HEADS * HGRN_EXPAND
HGRN_V_WIDTH = HGRN_HEADS * HGRN_HEAD_V
SPLITS = (ATTN_WIDTH, KV_WIDTH, KV_WIDTH, ATTN_WIDTH,
          HGRN_WIDTH, HGRN_WIDTH, HGRN_V_WIDTH, HGRN_V_WIDTH,
          D_MODEL, D_MODEL)
N_IN = int(sum(SPLITS))
SPLIT_POINTS = tuple(int(p) for p in np.cumsum(SPLITS)[:-1])
EPS = 1e-6

kernel_name = "hybrid_swa_sink_hgrn2_gated_merge"

def rmsnorm(x, gain):
    xf = x.astype(jnp.float32)
    y = xf * lax.rsqrt(jnp.mean(xf * xf, axis=-1, keepdims=True) + EPS)
    return (y * gain.astype(jnp.float32)).astype(x.dtype)

def _band(t, n_chunks):
    parts = [jnp.pad(t, ((0, 0), (j, 0), (0, 0), (0, 0), (0, 0)))[:, :n_chunks]
             for j in range(WIN_CHUNKS - 1, -1, -1)]
    return jnp.concatenate(parts, axis=2)

def window_sink_attention(q, k, v, sinks):
    B, S, _ = q.shape
    n_chunks = S // CHUNK
    grp = ATTN_Q_HEADS // ATTN_KV_HEADS
    qc = q.reshape(B, n_chunks, CHUNK, ATTN_KV_HEADS, grp, ATTN_HEAD_DIM)
    kb = _band(k.reshape(B, n_chunks, CHUNK, ATTN_KV_HEADS, ATTN_HEAD_DIM), n_chunks)
    vb = _band(v.reshape(B, n_chunks, CHUNK, ATTN_KV_HEADS, ATTN_HEAD_DIM), n_chunks)
    scale = ATTN_HEAD_DIM ** -0.5
    scores = jnp.einsum('bnckgd,bnmkd->bnkgcm', qc, kb).astype(jnp.float32) * scale
    shift = jnp.repeat(jnp.arange(WIN_CHUNKS - 1, -1, -1), CHUNK)
    valid = (jnp.arange(n_chunks)[:, None] - shift[None, :]) >= 0
    scores = jnp.where(valid[None, :, None, None, None, :], scores, -jnp.inf)
    sink = sinks.astype(jnp.float32).reshape(1, 1, ATTN_KV_HEADS, grp, 1, 1)
    m = jnp.maximum(jnp.max(scores, axis=-1, keepdims=True), sink)
    p = jnp.exp(scores - m)
    p = p / (jnp.sum(p, axis=-1, keepdims=True) + jnp.exp(sink - m))
    o = jnp.einsum('bnkgcm,bnmkd->bnckgd', p.astype(v.dtype), vb)
    return o.reshape(B, S, ATTN_WIDTH)

def hgrn2_chunkwise(q, f, i, lb):
    B, S, _ = q.shape
    n_chunks = S // CHUNK
    qf = jax.nn.silu(q.astype(jnp.float32))
    fg = lb + (1.0 - lb) * jax.nn.sigmoid(f.astype(jnp.float32))
    kf = 1.0 - fg
    gf = jnp.log(fg)
    vf = i.astype(jnp.float32)

    def to_chunks(t, d):
        return t.reshape(B, n_chunks, CHUNK, HGRN_HEADS, d).transpose(1, 0, 3, 2, 4)

    causal = jnp.tril(jnp.ones((CHUNK, CHUNK), dtype=bool))

    def step(state, xs):
        qc, kc, gc, vc = xs
        G = jnp.cumsum(gc, axis=2)
        diff = G[:, :, :, None, :] - G[:, :, None, :, :]
        decay = jnp.exp(jnp.where(causal[:, :, None], diff, -jnp.inf))
        attn = jnp.einsum('bhtk,bhsk,bhtsk->bhts', qc, kc, decay)
        o = (jnp.einsum('bhts,bhsv->bhtv', attn, vc)
             + jnp.einsum('bhtk,bhkv->bhtv', qc * jnp.exp(G), state))
        G_last = G[:, :, -1:, :]
        state = (jnp.exp(G_last[:, :, 0, :])[..., None] * state
                 + jnp.einsum('bhsk,bhsv->bhkv', kc * jnp.exp(G_last - G), vc))
        return state, o

    s0 = jnp.zeros((B, HGRN_HEADS, HGRN_EXPAND, HGRN_HEAD_V), jnp.float32)
    _, o = lax.scan(step, s0, (to_chunks(qf, HGRN_EXPAND), to_chunks(kf, HGRN_EXPAND),
                               to_chunks(gf, HGRN_EXPAND), to_chunks(vf, HGRN_HEAD_V)))
    return o.transpose(1, 0, 3, 2, 4).reshape(B, S, HGRN_HEADS, HGRN_HEAD_V)

def setup_inputs(seed: int = 0) -> dict:
    key = jax.random.key(seed)
    ks = jax.random.split(key, 10)
    f32 = jnp.float32
    x = jax.random.normal(ks[0], (BATCH, SEQ, D_MODEL), f32)
    norm_gain = 1.0 + 0.02 * jax.random.normal(ks[1], (DEPTH, D_MODEL), f32)
    w_in = jax.random.normal(ks[2], (DEPTH, D_MODEL, N_IN), f32) * D_MODEL ** -0.5
    attn_sinks = 0.5 * jax.random.normal(ks[3], (DEPTH, ATTN_Q_HEADS), f32)
    lb_logits = jax.random.normal(ks[4], (DEPTH + 1, HGRN_WIDTH), f32)
    hgrn_norm_gain = 1.0 + 0.02 * jax.random.normal(ks[5], (DEPTH, HGRN_V_WIDTH), f32)
    w_up_attn = jax.random.normal(ks[6], (DEPTH, ATTN_WIDTH, D_MODEL), f32) * ATTN_WIDTH ** -0.5
    w_up_hgrn = jax.random.normal(ks[7], (DEPTH, HGRN_V_WIDTH, D_MODEL), f32) * HGRN_V_WIDTH ** -0.5
    w_out = jax.random.normal(ks[8], (DEPTH, D_MODEL, D_MODEL), f32) * D_MODEL ** -0.5
    final_norm_gain = 1.0 + 0.02 * jax.random.normal(ks[9], (D_MODEL,), f32)
    return {"x": x, "norm_gain": norm_gain, "w_in": w_in, "attn_sinks": attn_sinks,
            "lb_logits": lb_logits, "hgrn_norm_gain": hgrn_norm_gain,
            "w_up_attn": w_up_attn, "w_up_hgrn": w_up_hgrn, "w_out": w_out,
            "final_norm_gain": final_norm_gain}

def reference(x, norm_gain, w_in, attn_sinks, lb_logits, hgrn_norm_gain,
              w_up_attn, w_up_hgrn, w_out, final_norm_gain):
    B, S, _ = x.shape
    lower_bounds = jnp.cumsum(jax.nn.softmax(lb_logits.astype(jnp.float32), axis=0), axis=0)
    for l in range(DEPTH):
        h = rmsnorm(x, norm_gain[l])
        proj = jnp.einsum('bsd,dn->bsn', h, w_in[l])
        qa, ka, va, za, qb, fb, ib, zb, ga, gb = jnp.split(proj, SPLIT_POINTS, axis=-1)
        a = window_sink_attention(qa, ka, va, attn_sinks[l]) * jax.nn.silu(za)
        ob = hgrn2_chunkwise(qb, fb, ib, lower_bounds[l])
        ob = ob * lax.rsqrt(jnp.mean(ob * ob, axis=-1, keepdims=True) + EPS)
        ob = ob.reshape(B, S, HGRN_V_WIDTH) * hgrn_norm_gain[l].astype(jnp.float32)
        b = ob.astype(x.dtype) * jax.nn.silu(zb)
        y = (jax.nn.sigmoid(ga) * jnp.einsum('bsc,cd->bsd', a, w_up_attn[l])
             + jax.nn.sigmoid(gb) * jnp.einsum('bsc,cd->bsd', b, w_up_hgrn[l]))
        x = x + jnp.einsum('bsd,de->bse', y, w_out[l])
    return rmsnorm(x, final_norm_gain)


_drawn_inputs = setup_inputs


def setup_inputs(seed=0):
    import zlib

    import numpy as np

    out = dict(_drawn_inputs(seed))
    spreads = {}
    factors = {'norm_gain': 5.871, 'attn_sinks': 8.0, 'hgrn_norm_gain': 8.0, 'final_norm_gain': 2.81}
    for name, (base, spread) in spreads.items():
        noise = np.random.default_rng([zlib.crc32(name.encode()), seed]).standard_normal(out[name].shape)
        drawn = base * np.exp(spread * noise) if base else spread * noise
        out[name] = __import__('jax').numpy.asarray(drawn.astype(out[name].dtype))
    for name, factor in factors.items():
        out[name] = (out[name] * factor).astype(out[name].dtype)
    return out
```

```python
from contextlib import ExitStack

import concourse.bass as bass
from concourse import mybir

P = 128
F32 = mybir.dt.float32
F32R = mybir.dt.float32r
ALU = mybir.AluOpType
ACT = mybir.ActivationFunctionType
AX_X = mybir.AxisListType.X

SEQ = 256
TT = SEQ // P
D = 4096
KT = D // P
HD = 128
HEADS = 16
KVH = 4
GH = 4
GROUPS = HEADS // GH
CHUNK = 64
CHUNKS = SEQ // CHUNK
BLK = GH * HD
WID = HEADS * HD
UT = WID // P
NB = D // BLK
EPS = 1e-6
SCALE = float(HD) ** -0.5

C_QA, C_KA, C_VA, C_ZA = 0, WID, WID + KVH * HD, WID + 2 * KVH * HD
C_QB = C_ZA + WID
C_FB, C_IB, C_ZB = C_QB + WID, C_QB + 2 * WID, C_QB + 3 * WID
C_GA = C_ZB + WID
C_GB = C_GA + D

HALVES = [CHUNK // 2 >> i for i in range(6)]
NL = len(HALVES)
L_G, L_END = NL, NL + 1

T_LEV = 0
T_AM = T_LEV + (NL + 1) * P
T_SCAN = T_AM + P + SEQ
T_ID = T_SCAN + SEQ
T_MEAN = T_ID + P
T_ALL = T_MEAN + P

RING = 4

N_HG = GROUPS * 4 * KT
N_KV = N_HG + 2 * KT
N_AT = N_KV + GROUPS * 2 * KT
N_GATE = 2 * KT + 2 * UT
N_MERGE = N_AT + NB * N_GATE


def count(base, per=0, it=0):
    def c(k=0, unit=1):
        if isinstance(it, int):
            return (base + per * it + k) // unit
        assert per % unit == 0
        return it * (per // unit) + (base + k) // unit
    return c


def build(nc, x, norm_gain, w_in, attn_sinks, lb_logits, hgrn_norm_gain, w_up_attn, w_up_hgrn,
          w_out, final_norm_gain, tables, out):
    ctx = ExitStack()
    with ctx:
        def sb(name, shape, dt=F32):
            return ctx.enter_context(nc.sbuf_tensor(name, shape, dt))

        def sem(name):
            return ctx.enter_context(nc.semaphore(name))

        raw = sb("raw", [P, RING, 2, BLK])
        w_hi = sb("w_hi", [P, RING, BLK], F32R)
        w_lo = sb("w_lo", [P, RING, BLK], F32R)
        h_hi = sb("h_hi", [P, KT, SEQ], F32R)
        h_lo = sb("h_lo", [P, KT, SEQ], F32R)
        region_base = nc.sbuf_base
        sb("branch_region", [P, 4 * UT * SEQ])
        proj_base = nc.sbuf_base
        sb("proj_region", [P, NB * GH * SEQ])
        k_att = sb("k_att", [P, GH, SEQ])
        v_att = sb("v_att", [P, TT, BLK])
        tab = sb("tab", [P, T_ALL])
        vec = sb("vec", [P, 80])
        lb = sb("lb", [P, HEADS])
        oml = sb("oml", [P, HEADS])
        sink = sb("sink", [P, HEADS])
        ssq = sb("ssq", [P, TT, NB])
        small = sb("small", [P, 16])
        eps_t = sb("eps_t", [P, 1])

        def at(base, name, shape, dt=F32):
            n = 4
            for s in shape[1:]:
                n *= s
            return nc.alloc_sbuf_tensor_at(name, shape, dt, offset=base), base + n

        a_hi, b1 = at(region_base, "a_hi", [P, UT, SEQ], F32R)
        a_lo, b2 = at(b1, "a_lo", [P, UT, SEQ], F32R)
        b_hi, b3 = at(b2, "b_hi", [P, UT, SEQ], F32R)
        b_lo, _ = at(b3, "b_lo", [P, UT, SEQ], F32R)
        decay, q = at(region_base, "decay", [P, NL + 2, SEQ])
        lev_m, q = at(q, "lev_m", [P, NL + 1, P])
        at_m, q = at(q, "at_m", [P, TT, P])
        fg, q = at(q, "fg", [P, SEQ])
        kf, q = at(q, "kf", [P, SEQ])
        gl, q = at(q, "gl", [P, SEQ])
        qg, q = at(q, "qg", [P, SEQ])
        kd_t, q = at(q, "kd_t", [P, TT, HD])
        iv, q = at(q, "iv", [P, TT, HD])
        state, q = at(q, "state", [P, CHUNKS - 1, HD])
        osq, q = at(q, "osq", [P, SEQ])
        lnm, q = at(q, "lnm", [P, SEQ])
        rs, q = at(q, "rs", [P, SEQ])
        bb1, q = at(q, "bb1", [P, SEQ])
        bb2, q = at(q, "bb2", [P, SEQ])
        assert q <= b2
        x_in, q = at(region_base, "x_in", [P, TT, D])
        vrow, q = at(q, "vrow", [80, P])
        xr, q = at(region_base, "xr", [P, TT, D])
        fgain, q = at(q, "fgain", [P, D])
        sq_o, q = at(q, "sq_o", [P, BLK])
        proj, _ = at(proj_base, "proj", [P, NB, GH * SEQ])
        sq_x, _ = at(proj_base, "sq_x", [P, D // 2])
        q = proj_base + 4 * 4 * GH * SEQ
        s_sb, q = at(q, "s_sb", [P, P + SEQ])
        p_t, q = at(q, "p_t", [P, 3, P])
        qw, q = at(q, "qw", [P, SEQ])
        vw, q = at(q, "vw", [P, TT, HD])
        aa, q = at(q, "aa", [P, SEQ])
        mx, q = at(q, "mx", [P, 8])
        negm, q = at(q, "negm", [P, 8])
        rowsum, q = at(q, "rowsum", [P, 8])
        esink, q = at(q, "esink", [P, 8])
        den, q = at(q, "den", [P, 8])
        rden, q = at(q, "rden", [P, 8])
        sig_b = k_att

        acc = ctx.enter_context(nc.psum_tensor("acc", [P, 2, 2 * BLK], F32))
        lev = ctx.enter_context(nc.psum_tensor("lev", [P, 2 * 512], F32))
        mis = ctx.enter_context(nc.psum_tensor("mis", [P, 512], F32))
        outp = ctx.enter_context(nc.psum_tensor("outp", [P, 512], F32))

        w_landed = [sem(f"w_landed{i}") for i in range(RING)]
        hi_ready = sem("hi_ready")
        lo_ready = sem("lo_ready")
        pe_done = sem("pe_done")
        tab_in, vec_in, sink_in = sem("tab_in"), sem("vec_in"), sem("sink_in")
        x_landed = [sem(f"x_landed{i}") for i in range(4)]
        eps_set = sem("eps_set")
        xsq = sem("xsq")
        xs_sum, xs_ln, xs_rs, x_scaled = sem("xs_sum"), sem("xs_ln"), sem("xs_rs"), sem("x_scaled")
        x_tr, h_hi_done, h_lo_done = sem("x_tr"), sem("h_hi_done"), sem("h_lo_done")
        vec_tr, vec_ready = sem("vec_tr"), sem("vec_ready")
        lb_chain, lb_exp, lb_ready = sem("lb_chain"), sem("lb_exp"), sem("lb_ready")
        e_neg, e_den, e_rec = sem("e_neg"), sem("e_den"), sem("e_rec")
        silu_done, i_copied, kv_copied, qa_copied = sem("silu_done"), sem("i_copied"), sem("kv_copied"), sem("qa_copied")
        fg_done, kf_done, ln_done, g_done = sem("fg_done"), sem("kf_done"), sem("ln_done"), sem("g_done")
        dec_args, dec_done, dec_mul, iv_done = sem("dec_args"), sem("dec_done"), sem("dec_mul"), sem("iv_done")
        kd_tr, kd_copied, levels_done = sem("kd_tr"), sem("kd_copied"), sem("levels_done")
        masked, att_done, kv_done = sem("masked"), sem("att_done"), sem("kv_done")
        st_done = [sem(f"st_done{i}") for i in range(CHUNKS - 1)]
        ho_done, osq_done, mean_done, lnm_done, rs_done = sem("ho_done"), sem("osq_done"), sem("mean_done"), sem("lnm_done"), sem("rs_done")
        bb1_done, bb2_done, b_hi_done, b_lo_done = sem("bb1_done"), sem("bb2_done"), sem("b_hi_done"), sem("b_lo_done")
        qvw_done, score_done, s_masked, mx_done, negm_done = sem("qvw_done"), sem("score_done"), sem("s_masked"), sem("mx_done"), sem("negm_done")
        p_exp, den_done, rden_done, p_norm = sem("p_exp"), sem("den_done"), sem("rden_done"), sem("p_norm")
        p_tr, pt_copied, pv_done, aa_done, a_hi_done, a_lo_done = sem("p_tr"), sem("pt_copied"), sem("pv_done"), sem("aa_done"), sem("a_hi_done"), sem("a_lo_done")
        sig_a_done, sig_b_done, ya_done, yb_part, y_done = sem("sig_a_done"), sem("sig_b_done"), sem("ya_done"), sem("yb_part"), sem("y_done")
        y_hi_done, y_lo_done = sem("y_hi_done"), sem("y_lo_done")
        xr_in, fgain_in = sem("xr_in"), sem("fgain_in")
        res_done, rsq_done, gained = sem("res_done"), sem("rsq_done"), sem("gained")
        fs_sum, fs_ln, fs_rs, fin_v, fin_s, stored = sem("fs_sum"), sem("fs_ln"), sem("fs_rs"), sem("fin_v"), sem("fin_s"), sem("stored")

        ident = tab[:, T_ID:T_ID + P]
        x_rows = x.rearrange("b (t p) d -> p (b t) d", p=P)
        out_rows = out.rearrange("b (t p) d -> p (b t) d", p=P)
        w_in_r = w_in.rearrange("l (c p) n -> p (l c) n", p=P)
        w_ua_r = w_up_attn.rearrange("l (c p) n -> p (l c) n", p=P)
        w_uh_r = w_up_hgrn.rearrange("l (c p) n -> p (l c) n", p=P)
        w_out_r = w_out.rearrange("l (c p) n -> p (l c) n", p=P)
        g_view = decay[:, L_G, :]
        kv_spot = [mis[:, 0:HD], outp[:, SEQ:SEQ + HD], mis[:, HD:2 * HD]]

        def heads(slot):
            return proj[:, bass.ds(slot, 1), :].rearrange("p one (h t) -> p (one h) t", h=GH)

        def flat(slot):
            return proj[:, bass.ds(slot, 1), :].rearrange("p one n -> p (one n)")

        def rows(slot):
            return proj[:, bass.ds(slot, 1), :].rearrange("p one (t n) -> p (one t) n", t=TT)

        block = ctx.enter_context(nc.Block())

        @block.sync
        def _(sp):
            for t in range(TT):
                for half in range(2):
                    cols = slice(half * (D // 2), (half + 1) * (D // 2))
                    sp.dma_start(x_in[:, t, cols], x_rows[:, t, cols]).then_inc(x_landed[2 * t + half], 16)
                if t == 0:
                    sp.dma_start(vrow[0:32, :], norm_gain.rearrange("a (c p) -> (a c) p", p=P)).then_inc(vec_in, 16)
                    sp.dma_start(vrow[32:64, :], lb_logits.rearrange("a (c p) -> (a c) p", p=P)).then_inc(vec_in, 16)
                    sp.dma_start(vrow[64:80, :], hgrn_norm_gain.rearrange("a (c p) -> (a c) p", p=P)).then_inc(vec_in, 16)
                    sp.dma_start(sink[:, :], attn_sinks.broadcast_to([P, HEADS])).then_inc(sink_in, 16)
                    sp.dma_start(tab[:, :], tables).then_inc(tab_in, 16)

            def load_steps(n, w, col, steps, fresh=0):
                with sp.Fori(0, steps // (2 * RING)) as c:
                    for r in range(RING):
                        if not fresh:
                            sp.wait_ge(lo_ready, c * (2 * RING) + n(2 * r - 2 * RING + 2))
                        sp.dma_start(raw[:, r, :, :], w[:, bass.ds(c * (2 * RING) + 2 * r, 2), bass.ds(col, BLK)]
                                     ).then_inc(w_landed[r], 16)

            def load_first(w, col):
                for r in range(RING):
                    sp.dma_start(raw[:, r, :, :], w[:, 2 * r:2 * r + 2, bass.ds(col, BLK)]).then_inc(w_landed[r], 16)
                with sp.Fori(1, KT // (2 * RING)) as c:
                    for r in range(RING):
                        sp.wait_ge(lo_ready, c * (2 * RING) + (2 * r - 2 * RING + 2))
                        sp.dma_start(raw[:, r, :, :], w[:, bass.ds(c * (2 * RING) + 2 * r, 2), bass.ds(col, BLK)]
                                     ).then_inc(w_landed[r], 16)

            load_first(w_in_r, C_FB)
            for b, c0 in ((1, C_QB), (2, C_IB), (3, C_ZB)):
                load_steps(count(b * KT), w_in_r, c0, KT)
            with sp.Fori(1, GROUPS) as g:
                for b, c0 in enumerate((C_FB, C_QB, C_IB, C_ZB)):
                    load_steps(count(b * KT, 4 * KT, g), w_in_r, g * BLK + c0, KT)
            load_steps(count(N_HG), w_in_r, C_KA, KT)
            load_steps(count(N_HG + KT), w_in_r, C_VA, KT)
            with sp.Fori(0, GROUPS) as g:
                for b, c0 in enumerate((C_QA, C_ZA)):
                    load_steps(count(N_KV + b * KT, 2 * KT, g), w_in_r, g * BLK + c0, KT)
            with sp.Fori(0, NB) as j:
                load_steps(count(N_AT, N_GATE, j), w_in_r, j * BLK + C_GA, KT)
                load_steps(count(N_AT + KT, N_GATE, j), w_in_r, j * BLK + C_GB, KT)
                load_steps(count(N_AT + 2 * KT, N_GATE, j), w_ua_r, j * BLK, UT)
                load_steps(count(N_AT + 2 * KT + UT, N_GATE, j), w_uh_r, j * BLK, UT)
            load_steps(count(N_MERGE), w_out_r, 0, KT)
            sp.wait_ge(pe_done, N_MERGE)
            sp.dma_start(xr[:, :, :], x_rows).then_inc(xr_in, 16)
            sp.dma_start(fgain[:, :], final_norm_gain.rearrange("(a d) -> a d", a=1).broadcast_to([P, D])).then_inc(fgain_in, 16)
            with sp.Fori(1, NB) as n:
                load_steps(count(N_MERGE, KT, n), w_out_r, n * BLK, KT)
            for i in range(4):
                cols = slice(i * (D // 4), (i + 1) * (D // 4))
                sp.wait_ge(fin_v, i + 1)
                sp.dma_start(out_rows[:, 0, cols], xr[:, 0, cols]).then_inc(stored, 16)
                sp.wait_ge(fin_s, i + 1)
                sp.dma_start(out_rows[:, 1, cols], xr[:, 1, cols]).then_inc(stored, 16)
            sp.wait_ge(stored, 8 * 16)

        @block.tensor
        def _(pe):
            def step_t(n, k, par, r_hi, r_lo, kt, last, free):
                s = k % RING
                if kt == 0 and free is not None:
                    pe.wait_ge(*free)
                pe.wait_ge(lo_ready, n(k + 1))
                for c in range(GH):
                    o = acc[:, par, c * SEQ:(c + 1) * SEQ]
                    cols = slice(c * HD, (c + 1) * HD)
                    first = kt == 0 and c % 2 == 0
                    nc.tensor.matmul(o, w_hi[:, s, cols], r_hi[:, kt, :], start=first, stop=False)
                    nc.tensor.matmul(o, w_hi[:, s, cols], r_lo[:, kt, :], start=False, stop=False)
                    m = nc.tensor.matmul(o, w_lo[:, s, cols], r_hi[:, kt, :], start=False, stop=last and c % 2 == 1)
                m.then_inc(pe_done, 1)

            def step_r(n, k, par, kt, last, free):
                s = k % RING
                if kt == 0 and free is not None:
                    pe.wait_ge(*free)
                pe.wait_ge(lo_ready, n(k + 1))
                for t in range(TT):
                    o = acc[:, par, t * BLK:(t + 1) * BLK]
                    tok = slice(t * P, (t + 1) * P)
                    nc.tensor.matmul(o, h_hi[:, kt, tok], w_hi[:, s, :], start=kt == 0, stop=False)
                    nc.tensor.matmul(o, h_lo[:, kt, tok], w_hi[:, s, :], start=False, stop=False)
                    m = nc.tensor.matmul(o, h_hi[:, kt, tok], w_lo[:, s, :], start=False, stop=last)
                m.then_inc(pe_done, 1)

            def levels(t, head):
                tok = slice(t * P, (t + 1) * P)
                for i in range(NL):
                    nc.tensor.matmul(lev[:, i * P:(i + 1) * P], decay[:, i, tok], decay[:, i, tok], start=True, stop=True)
                return tok

            def hgrn_side(k, hd, slot, b):
                if k == 9:
                    pe.wait_ge(dec_mul, hd(1))
                    for t in range(TT):
                        m = nc.tensor.transpose(mis[:, t * P:(t + 1) * P], decay[:, L_END, t * P:(t + 1) * P], ident)
                    m.then_inc(kd_tr, 1)
                if k == 9 or k == 14:
                    t = (k - 9) // 5
                    if t:
                        pe.wait_ge(masked, hd(0) * 2 + 1)
                    tok = levels(t, hd)
                    nc.tensor.matmul(lev[:, NL * P:(NL + 1) * P], kf[:, tok], heads(slot + 1)[:, b, tok],
                                     start=True, stop=True).then_inc(levels_done, 1)
                if k == 14:
                    pe.wait_ge(kd_copied, hd(1))
                    pe.wait_ge(iv_done, hd(1))
                    for c in range(CHUNKS - 1):
                        part = slice((c % 2) * CHUNK, (c % 2 + 1) * CHUNK)
                        m = nc.tensor.matmul(kv_spot[c], kd_t[part, c // 2, :], iv[part, c // 2, :],
                                             start=True, stop=True)
                    m.then_inc(kv_done, 1)
                if k == 19:
                    pe.wait_ge(att_done, hd(0) * 2 + 2)
                    pe.wait_ge(st_done[-1], hd(1))
                    for t in range(TT):
                        nc.tensor.matmul(outp[:, t * P:(t + 1) * P], iv[:, t, :], at_m[:, t, :], start=True, stop=False)
                        for c in range(max(1, 2 * t), 2 * t + 2):
                            cols = slice(c * CHUNK, (c + 1) * CHUNK)
                            m = nc.tensor.matmul(outp[:, cols], state[:, c - 1, :], qg[:, cols],
                                                 start=False, stop=c == 2 * t + 1)
                    m.then_inc(ho_done, 1)
                if k == 24:
                    pe.wait_ge(osq_done, hd(1))
                    nc.tensor.matmul(outp[:, SEQ:2 * SEQ], tab[:, T_MEAN:T_MEAN + P], osq[:, :],
                                     start=True, stop=True).then_inc(mean_done, 1)

            def attn_side(k, hd, g):
                if k == 1:
                    pe.wait_ge(qvw_done, hd(1))
                    keys = k_att[:, bass.ds(g, 1), :].rearrange("p one t -> p (one t)")
                    nc.tensor.matmul(lev[:, 0:P], qw[:, 0:P], keys[:, 0:P], start=True, stop=True)
                    nc.tensor.matmul(lev[:, P:P + SEQ], qw[:, P:SEQ], keys, start=True, stop=True).then_inc(score_done, 1)
                if k == 6:
                    pe.wait_ge(p_norm, hd(1))
                    for i in range(3):
                        m = nc.tensor.transpose(mis[:, i * P:(i + 1) * P], s_sb[:, i * P:(i + 1) * P], ident)
                    m.then_inc(p_tr, 1)
                if k == 10:
                    pe.wait_ge(pt_copied, hd(1))
                    nc.tensor.matmul(outp[:, 0:P], vw[:, 0, :], p_t[:, 0, :], start=True, stop=True)
                    nc.tensor.matmul(outp[:, P:SEQ], vw[:, 0, :], p_t[:, 1, :], start=True, stop=False)
                    nc.tensor.matmul(outp[:, P:SEQ], vw[:, 1, :], p_t[:, 2, :], start=False, stop=True).then_inc(pv_done, 1)

            pe.wait_ge(vec_in, 48)
            pe.wait_ge(tab_in, 16)
            nc.tensor.transpose(outp[:, 0:80], vrow[0:80, :], ident[0:80, 0:80]).then_inc(vec_tr, 1)
            pe.wait_ge(x_scaled, TT)
            pe.wait_ge(vec_ready, 1)
            spots = [lev[:, 0:512], lev[:, 512:1024], mis[:, :], outp[:, :]]
            for p in range(KT // 2):
                if p >= 4:
                    pe.wait_ge(h_lo_done, p - 3)
                for i in range(2):
                    for t in range(TT):
                        kt = 2 * p + i
                        m = nc.tensor.transpose(spots[p % 4][:, (i * TT + t) * P:(i * TT + t + 1) * P],
                                                x_in[:, t, kt * P:(kt + 1) * P], ident)
                m.then_inc(x_tr, 1)

            def hgrn_group(n, g, hd, slot, side):
                before = [(i_copied, g), (silu_done, g * 2), (e_neg, g * 3 + 1), (silu_done, g * 2 + 1)]
                for b in range(4):
                    free = before[b] if side or b >= 2 else None
                    for k in range(KT):
                        kk = b * KT + k
                        if b == 2:
                            step_r(n, kk, b % 2, k, k == KT - 1, free)
                        else:
                            step_t(n, kk, b % 2, h_hi, h_lo, k, k == KT - 1, free)
                        if side:
                            hgrn_side(k, lambda i, b=b: hd(b + i), slot, b)

            pe.wait_ge(h_lo_done, KT // 2)
            hgrn_group(count(0), 0, None, None, False)
            with pe.Fori(1, GROUPS) as g:
                hgrn_group(count(0, 4 * KT, g), g, count(-GH, GH, g), ((g + 1) % 2) * 4, True)

            last_set = ((GROUPS - 1) % 2) * 4
            n = count(N_HG)
            before = [(i_copied, GROUPS), (silu_done, 2 * GROUPS), (kv_copied, 1), (kv_copied, 2)]
            for b in range(4):
                for k in range(KT):
                    kk = b * KT + k
                    free = before[b]
                    if b == 1:
                        step_r(n, kk, b % 2, k, k == KT - 1, free)
                    else:
                        step_t(n, kk, b % 2, h_hi, h_lo, k, k == KT - 1, free)
                    hgrn_side(k, lambda i, b=b: (GROUPS - 1) * GH + b + i, last_set, b)

            def attn_blocks(n, hd, g):
                before = [(qa_copied, g + 1), (silu_done, g + (2 * GROUPS + 1))]
                for b in range(2):
                    for k in range(KT):
                        kk = b * KT + k
                        step_t(n, kk, b % 2, h_hi, h_lo, k, k == KT - 1, before[b])
                        attn_side(k % 16, lambda i, u=kk // 16: hd(u + i), g)

            with pe.Fori(1, GROUPS) as g:
                attn_blocks(count(N_KV, 2 * KT, g), count(-GH, GH, g), g - 1)

            def merge(n, j, side):
                before = [(qa_copied, GROUPS), (silu_done, 3 * GROUPS)] if side else [(ya_done, j), (yb_part, j)]
                for k in range(2 * KT):
                    step_t(n, k, k // KT, h_hi, h_lo, k % KT, k % KT == KT - 1, before[k // KT])
                    if side:
                        attn_side(k % 16, lambda i, u=k // 16: (GROUPS - 1) * GH + u + i, GROUPS - 1)
                if side:
                    pe.wait_ge(a_lo_done, HEADS)
                    pe.wait_ge(b_lo_done, HEADS)
                for k in range(UT):
                    step_t(n, 2 * KT + k, 0, a_hi, a_lo, k, k == UT - 1, (sig_a_done, j + 1))
                for k in range(UT):
                    step_t(n, 2 * KT + UT + k, 1, b_hi, b_lo, k, k == UT - 1, (sig_b_done, j + 1))

            merge(count(N_AT), 0, True)
            with pe.Fori(1, NB) as j:
                merge(count(N_AT, N_GATE, j), j, False)

            def project(n, before, first):
                for b in range(2):
                    for k in range(KT):
                        if first and b == 0 and k % GH == 0:
                            pe.wait_ge(y_lo_done, k // GH + 1)
                        step_r(n, b * KT + k, b, k, k == KT - 1, before[b])

            project(count(N_MERGE), [(ya_done, NB), (yb_part, NB)], True)
            with pe.Fori(1, NB // 2) as m:
                project(count(N_MERGE, 2 * KT, m), [(res_done, m * 2 - 1), (res_done, m * 2)], False)

        @block.scalar
        def _(act):
            def round_step(n, k, fresh=False):
                if k % 2 == 0:
                    act.wait_ge(w_landed[(k // 2) % RING], (n(k, 2 * RING) + 1) * 16)
                if not (fresh and k < RING):
                    act.wait_ge(pe_done, n(k - RING + 1))
                nc.scalar.activation(w_hi[:, k % RING, :], raw[:, (k // 2) % RING, k % 2, :], ACT.Copy).then_inc(hi_ready, 1)

            def exp_neg(dst, par, n_end):
                act.wait_ge(pe_done, n_end)
                nc.scalar.activation(dst, acc[:, par, :], ACT.Exp, scale=-1.0).then_inc(e_neg, 1)

            def hgrn_epilogue(b, par, n_end, slot):
                if b == 2:
                    act.wait_ge(pe_done, n_end)
                    nc.scalar.activation(flat(slot + 2), acc[:, par, :], ACT.Copy).then_inc(i_copied, 1)
                else:
                    exp_neg(flat(slot + b), par, n_end)

            def hgrn_side(k, hd, g1, slot, b):
                if k == 1:
                    if b == 0:
                        act.wait_ge(i_copied, g1)
                    nc.scalar.activation(iv[:, :, :], rows(slot + 2)[:, :, b * HD:(b + 1) * HD], ACT.Copy).then_inc(iv_done, 1)
                if k == 3:
                    act.wait_ge(fg_done, hd(1))
                    nc.scalar.activation(gl[:, :], fg[:, :], ACT.Ln).then_inc(ln_done, 1)
                if k == 6:
                    act.wait_ge(dec_args, hd(1))
                    nc.scalar.activation(decay[:, :, :], decay[:, :, :], ACT.Exp).then_inc(dec_done, 1)
                if k == 13:
                    act.wait_ge(kd_tr, hd(1))
                    nc.scalar.activation(kd_t[:, :, :], mis[:, 0:TT * P].rearrange("p (t d) -> p t d", t=TT), ACT.Copy
                                         ).then_inc(kd_copied, 1)
                if k == 22:
                    act.wait_ge(ho_done, hd(1))
                    nc.scalar.activation(osq[:, :], outp[:, 0:SEQ], ACT.Square).then_inc(osq_done, 1)
                if k == 27:
                    act.wait_ge(mean_done, hd(1))
                    act.wait_ge(eps_set, 1)
                    nc.scalar.activation(lnm[:, :], outp[:, SEQ:2 * SEQ], ACT.Ln, bias=eps_t[:, :]).then_inc(lnm_done, 1)
                    act.wait_ge(lnm_done, hd(1))
                    nc.scalar.activation(rs[:, :], lnm[:, :], ACT.Exp, scale=-0.5).then_inc(rs_done, 1)
                if k == 29:
                    act.wait_ge(bb2_done, hd(1))
                    nc.scalar.activation(b_hi[:, bass.ds(hd(0), 1), :].rearrange("p one t -> p (one t)"), bb2[:, :], ACT.Copy
                                         ).then_inc(b_hi_done, 1)

            def attn_side(k, hd, g):
                if k == 4:
                    act.wait_ge(negm_done, hd(1))
                    cuts = (slice(0, P), slice(P, P + SEQ))
                    for t in range(TT):
                        nc.scalar.activation(s_sb[:, cuts[t]], s_sb[:, cuts[t]], ACT.Exp, bias=negm[:, t:t + 1],
                                             accum_out=rowsum[:, t:t + 1])
                    nc.scalar.activation(esink[:, 0:TT], negm[:, 0:TT], ACT.Exp, bias=sink[:, bass.ds(hd(0), 1)]).then_inc(p_exp, 1)
                if k == 9:
                    act.wait_ge(p_tr, hd(1))
                    nc.scalar.activation(p_t[:, :, :], mis[:, 0:3 * P].rearrange("p (i t) -> p i t", i=3), ACT.Copy).then_inc(pt_copied, 1)
                if k == 14:
                    act.wait_ge(aa_done, hd(1))
                    nc.scalar.activation(a_hi[:, bass.ds(hd(0), 1), :].rearrange("p one t -> p (one t)"), aa[:, :], ACT.Copy
                                         ).then_inc(a_hi_done, 1)

            def attn_load(k, hd, g, qslot, b):
                if k == 0:
                    act.wait_ge(qa_copied, g + 1)
                    act.wait_ge(kv_copied, 2)
                    nc.scalar.activation(qw[:, :], heads(qslot)[:, b, :], ACT.Copy, scale=SCALE)
                    nc.scalar.activation(vw[:, :, :], v_att[:, :, bass.ds(g * HD, HD)], ACT.Copy).then_inc(qvw_done, 1)

            act.wait_ge(sink_in, 16)
            for i in range(4):
                act.wait_ge(x_landed[i], 16)
                if i:
                    act.wait_ge(xsq, i)
                nc.scalar.activation(sq_x[:, :], x_in[:, i // 2, (i % 2) * (D // 2):(i % 2 + 1) * (D // 2)], ACT.Square,
                                     accum_out=small[:, i:i + 1]).then_inc(xsq, 1)
            act.wait_ge(xs_sum, 1)
            act.wait_ge(eps_set, 1)
            nc.scalar.activation(small[:, 6:8], small[:, 4:6], ACT.Ln, scale=1.0 / D, bias=eps_t[:, :]).then_inc(xs_ln, 1)
            act.wait_ge(xs_ln, 1)
            nc.scalar.activation(small[:, 8:10], small[:, 6:8], ACT.Exp, scale=-0.5).then_inc(xs_rs, 1)
            spots = [lev[:, 0:512], lev[:, 512:1024], mis[:, :], outp[:, :]]
            act.wait_ge(vec_ready, 1)
            for p in range(KT // 2):
                act.wait_ge(x_tr, p + 1)
                for i in range(2):
                    kt = 2 * p + i
                    m = nc.scalar.activation(h_hi[:, kt, :], spots[p % 4][:, i * SEQ:(i + 1) * SEQ], ACT.Copy, scale=vec[:, kt:kt + 1])
                m.then_inc(h_hi_done, 1)
            act.wait_ge(lb_chain, 2)
            nc.scalar.activation(lnm[:, 0:32], lnm[:, 0:32], ACT.Exp).then_inc(lb_exp, 1)

            def hgrn_group(n, hd, g, slot, prev_slot, side, first=False):
                for b in range(4):
                    for k in range(KT):
                        kk = b * KT + k
                        round_step(n, kk, fresh=first)
                        if k == 3 and not (first and b == 0):
                            pb = (b - 1) % 4
                            hgrn_epilogue(pb, pb % 2, n(b * KT), slot if b else prev_slot)
                        if side:
                            hgrn_side(k, lambda i, b=b: hd(b + i), g, prev_slot, b)

            hgrn_group(count(0), None, 0, 0, 4, False, first=True)
            with act.Fori(1, GROUPS) as g:
                hgrn_group(count(0, 4 * KT, g), count(-GH, GH, g), g, (g % 2) * 4, ((g + 1) % 2) * 4, True)

            last_set = ((GROUPS - 1) % 2) * 4
            n = count(N_HG)
            for b in range(4):
                for k in range(KT):
                    round_step(n, b * KT + k)
                    if k == 3:
                        if b == 0:
                            hgrn_epilogue(3, 1, n(0), last_set)
                        elif b == 1:
                            act.wait_ge(pe_done, n(KT))
                            nc.scalar.activation(k_att[:, :, :], acc[:, 0, :].rearrange("p (h t) -> p h t", h=GH), ACT.Copy).then_inc(kv_copied, 1)
                        elif b == 2:
                            act.wait_ge(pe_done, n(2 * KT))
                            nc.scalar.activation(v_att[:, :, :], acc[:, 1, :].rearrange("p (t c) -> p t c", t=TT), ACT.Copy).then_inc(kv_copied, 1)
                        else:
                            act.wait_ge(pe_done, n(3 * KT))
                            nc.scalar.activation(flat(0), acc[:, 0, :], ACT.Copy).then_inc(qa_copied, 1)
                    hgrn_side(k, lambda i, b=b: (GROUPS - 1) * GH + b + i, GROUPS, last_set, b)

            with act.Fori(1, GROUPS) as g:
                n = count(N_KV, 2 * KT, g)
                hd = count(-GH, GH, g)
                for b in range(2):
                    for k in range(KT):
                        kk = b * KT + k
                        round_step(n, kk)
                        attn_load(k % 16, lambda i, u=kk // 16: hd(u + i), g - 1, ((g + 1) % 2) * 2, kk // 16)
                        if k == 3 and b == 0:
                            exp_neg(flat(((g + 1) % 2) * 2 + 1), 1, n(0))
                        if k == 3 and b == 1:
                            act.wait_ge(pe_done, n(KT))
                            nc.scalar.activation(flat((g % 2) * 2), acc[:, 0, :], ACT.Copy).then_inc(qa_copied, 1)
                        attn_side(k % 16, lambda i, u=kk // 16: hd(u + i), g - 1)

            def merge(n, j, side):
                for k in range(N_GATE):
                    round_step(n, k)
                    if side and k < 2 * KT:
                        h0 = (GROUPS - 1) * GH + k // 16
                        attn_load(k % 16, lambda i: h0 + i, GROUPS - 1, ((GROUPS - 1) % 2) * 2, k // 16)
                        if k == 3:
                            exp_neg(flat(((GROUPS - 1) % 2) * 2 + 1), 1, n(0))
                        attn_side(k % 16, lambda i: h0 + i, GROUPS - 1)
                    if k == KT + 3:
                        act.wait_ge(pe_done, n(KT))
                        nc.scalar.activation(flat(j), acc[:, 0, :], ACT.Sigmoid).then_inc(sig_a_done, 1)
                    if k == 2 * KT + 3:
                        act.wait_ge(pe_done, n(2 * KT))
                        nc.scalar.activation(sig_b[:, :, :], acc[:, 1, :].rearrange("p (h t) -> p h t", h=GH), ACT.Sigmoid).then_inc(sig_b_done, 1)

            merge(count(N_AT), 0, True)
            with act.Fori(1, NB) as j:
                merge(count(N_AT, N_GATE, j), j, False)

            def project(n, first, a):
                for b in range(2):
                    for k in range(KT):
                        if first and b == 0 and k % GH == 0:
                            j = k // GH
                            act.wait_ge(y_done, j + 1)
                            nc.scalar.activation(h_hi[:, j * GH:(j + 1) * GH, :], heads(j), ACT.Copy).then_inc(y_hi_done, 1)
                        round_step(n, b * KT + k)
                        if k == 6 and not (first and b == 0):
                            squares(a(b - 1))

            def squares(i):
                act.wait_ge(res_done, i + 1)
                for t in range(TT):
                    m = nc.scalar.activation(sq_o[:, :], xr[:, t, bass.ds(i * BLK, BLK)], ACT.Square,
                                             accum_out=ssq[:, t, bass.ds(i, 1)])
                    m.then_inc(rsq_done, 1)
                    act.wait_ge(rsq_done, i * 2 + (t + 1))

            project(count(N_MERGE), True, count(0))
            with act.Fori(1, NB // 2) as m:
                project(count(N_MERGE, 2 * KT, m), False, count(0, 2, m))
            squares(NB - 1)
            act.wait_ge(fs_sum, 1)
            nc.scalar.activation(small[:, 2:4], small[:, 0:2], ACT.Ln, scale=1.0 / D, bias=eps_t[:, :]).then_inc(fs_ln, 1)
            act.wait_ge(fs_ln, 1)
            nc.scalar.activation(small[:, 4:6], small[:, 2:4], ACT.Exp, scale=-0.5).then_inc(fs_rs, 1)
            act.wait_ge(fs_rs, 1)
            act.wait_ge(gained, NB)
            for i in range(4):
                cols = slice(i * (D // 4), (i + 1) * (D // 4))
                nc.scalar.activation(xr[:, 1, cols], xr[:, 1, cols], ACT.Copy, scale=small[:, 5:6]).then_inc(fin_s, 1)

        @block.vector
        def _(dve):
            def rest_step(n, k):
                dve.wait_ge(hi_ready, n(k + 1))
                nc.vector.tensor_tensor(w_lo[:, k % RING, :], raw[:, (k // 2) % RING, k % 2, :],
                                        w_hi[:, k % RING, :].bitcast(F32), ALU.subtract).then_inc(lo_ready, 1)

            def sigmoid_parts(k, buf, e, par, silu):
                q4 = GH * SEQ // 4
                if k == 4:
                    dve.wait_ge(e_neg, e + 1)
                    nc.vector.tensor_scalar(buf, buf, 1.0, None, ALU.add).then_inc(e_den, 1)
                    dve.wait_ge(e_den, e + 1)
                for i in range(4):
                    if k == 5 + 2 * i:
                        m = nc.vector.reciprocal(buf[:, i * q4:(i + 1) * q4], buf[:, i * q4:(i + 1) * q4])
                        if i == 3:
                            m.then_inc(e_rec, 1)
                if k == 12 and silu is not None:
                    dve.wait_ge(e_rec, e + 1)
                    nc.vector.tensor_tensor(buf, buf, acc[:, par, :], ALU.mult).then_inc(silu_done, 1)

            def hgrn_side(k, hd, f_count, z_count, slot, b):
                if k == 2:
                    dve.wait_ge(e_rec, f_count)
                    dve.wait_ge(lb_ready, 2)
                    f = heads(slot)[:, b, :]
                    nc.vector.tensor_scalar(fg[:, :], f, oml[:, bass.ds(hd(0), 1)], lb[:, bass.ds(hd(0), 1)], ALU.mult, ALU.add).then_inc(fg_done, 1)
                    dve.wait_ge(fg_done, hd(1))
                    nc.vector.tensor_scalar(kf[:, :], fg[:, :], -1.0, 1.0, ALU.mult, ALU.add).then_inc(kf_done, 1)
                if k == 4:
                    dve.wait_ge(ln_done, hd(1))
                    nc.vector.tensor_tensor_scan(g_view, tab[:, T_SCAN:T_SCAN + SEQ], gl[:, :], 0.0, ALU.mult, ALU.add).then_inc(g_done, 1)
                if k in (4, 5):
                    if k == 4:
                        dve.wait_ge(g_done, hd(1))
                    for i in range(NL)[slice(0, 3) if k == 4 else slice(3, NL)]:
                        m = HALVES[i]
                        gv = g_view.rearrange("p (c two m) -> p c two m", two=2, m=m)
                        dv = decay[:, i, :].rearrange("p (c two m) -> p c two m", two=2, m=m)
                        mid = gv[:, :, 0, m - 1:m].broadcast_to([P, SEQ // (2 * m), m])
                        nc.vector.tensor_tensor(dv[:, :, 0, :], mid, gv[:, :, 0, :], ALU.subtract)
                        nc.vector.tensor_tensor(dv[:, :, 1, :], gv[:, :, 1, :], mid, ALU.subtract)
                    if k == 5:
                        gv = g_view.rearrange("p (c t) -> p c t", t=CHUNK)
                        end = gv[:, :, CHUNK - 1:CHUNK].broadcast_to([P, CHUNKS, CHUNK])
                        nc.vector.tensor_tensor(decay[:, L_END, :].rearrange("p (c t) -> p c t", t=CHUNK), end, gv,
                                                ALU.subtract).then_inc(dec_args, 1)
                if k in (7, 8):
                    qh = heads(slot + 1)[:, b, :]
                    if k == 7:
                        dve.wait_ge(dec_done, hd(1))
                        dve.wait_ge(kf_done, hd(1))
                        dve.wait_ge(silu_done, z_count - 1)
                    for i in range(NL)[slice(0, 3) if k == 7 else slice(3, NL)]:
                        m = HALVES[i]
                        dv = decay[:, i, :].rearrange("p (c two m) -> p c two m", two=2, m=m)
                        kv = kf[:, :].rearrange("p (c two m) -> p c two m", two=2, m=m)
                        qv = qh.rearrange("p (c two m) -> p c two m", two=2, m=m)
                        nc.vector.tensor_tensor(dv[:, :, 0, :], dv[:, :, 0, :], kv[:, :, 0, :], ALU.mult)
                        nc.vector.tensor_tensor(dv[:, :, 1, :], dv[:, :, 1, :], qv[:, :, 1, :], ALU.mult)
                    if k == 8:
                        nc.vector.tensor_tensor(qg[:, :], g_view, qh, ALU.mult)
                        nc.vector.tensor_tensor(decay[:, L_END, :], decay[:, L_END, :], kf[:, :], ALU.mult).then_inc(dec_mul, 1)
                if k in (12, 18):
                    t = (k - 12) // 6
                    dve.wait_ge(levels_done, hd(0) * 2 + (t + 1))
                    nc.vector.tensor_tensor(lev_m[:, :, :], lev[:, 0:(NL + 1) * P].rearrange("p (l t) -> p l t", t=P),
                                            tab[:, T_LEV:T_LEV + (NL + 1) * P].rearrange("p (l t) -> p l t", t=P),
                                            ALU.mult).then_inc(masked, 1)
                    dve.wait_ge(masked, hd(0) * 2 + (t + 1))
                    nc.vector.tensor_reduce(at_m[:, t, :], lev_m[:, :, :].rearrange("p l t -> p t l"), AX_X, ALU.add).then_inc(att_done, 1)
                if k == 17:
                    dve.wait_ge(kv_done, hd(1))
                    nc.vector.tensor_copy(state[:, 0, :], kv_spot[0]).then_inc(st_done[0], 1)
                    for c in range(1, CHUNKS - 1):
                        dve.wait_ge(st_done[c - 1], hd(1))
                        end = g_view[:, c * CHUNK + CHUNK - 1:c * CHUNK + CHUNK]
                        nc.vector.scalar_tensor_tensor(state[:, c, :], state[:, c - 1, :], end, kv_spot[c],
                                                       ALU.mult, ALU.add).then_inc(st_done[c], 1)
                if k == 28:
                    dve.wait_ge(rs_done, hd(1))
                    nc.vector.scalar_tensor_tensor(bb1[:, :], outp[:, 0:SEQ], vec[:, bass.ds(hd(64), 1)], rs[:, :],
                                                   ALU.mult, ALU.mult).then_inc(bb1_done, 1)
                    dve.wait_ge(bb1_done, hd(1))
                    dve.wait_ge(silu_done, z_count)
                    nc.vector.tensor_tensor(bb2[:, :], bb1[:, :], heads(slot + 3)[:, b, :], ALU.mult).then_inc(bb2_done, 1)
                if k == 29:
                    dve.wait_ge(b_hi_done, hd(1))
                    hi = b_hi[:, bass.ds(hd(0), 1), :].rearrange("p one t -> p (one t)").bitcast(F32)
                    nc.vector.tensor_tensor(b_lo[:, bass.ds(hd(0), 1), :].rearrange("p one t -> p (one t)"), bb2[:, :], hi,
                                            ALU.subtract).then_inc(b_lo_done, 1)

            def attn_side(k, hd, z_count, zslot, b):
                cuts = (slice(0, P), slice(P, P + SEQ))
                if k == 4:
                    dve.wait_ge(score_done, hd(1))
                    nc.vector.tensor_tensor(s_sb[:, :], lev[:, 0:P + SEQ], tab[:, T_AM:T_AM + P + SEQ], ALU.add).then_inc(s_masked, 1)
                    dve.wait_ge(s_masked, hd(1))
                    nc.vector.reduce_max(mx[:, 0:1], s_sb[:, cuts[0]], AX_X)
                    nc.vector.reduce_max(mx[:, 1:2], s_sb[:, cuts[1]], AX_X).then_inc(mx_done, 1)
                    dve.wait_ge(mx_done, hd(1))
                    nc.vector.tensor_scalar(negm[:, 0:TT], mx[:, 0:TT], sink[:, bass.ds(hd(0), 1)], -1.0, ALU.max, ALU.mult
                                            ).then_inc(negm_done, 1)
                if k == 5:
                    dve.wait_ge(p_exp, hd(1))
                    nc.vector.tensor_tensor(den[:, 0:TT], rowsum[:, 0:TT], esink[:, 0:TT], ALU.add).then_inc(den_done, 1)
                    dve.wait_ge(den_done, hd(1))
                    nc.vector.reciprocal(rden[:, 0:TT], den[:, 0:TT]).then_inc(rden_done, 1)
                    dve.wait_ge(rden_done, hd(1))
                    nc.vector.tensor_scalar(s_sb[:, cuts[0]], s_sb[:, cuts[0]], rden[:, 0:1], None, ALU.mult)
                    nc.vector.tensor_scalar(s_sb[:, cuts[1]], s_sb[:, cuts[1]], rden[:, 1:2], None, ALU.mult).then_inc(p_norm, 1)
                if k == 13:
                    dve.wait_ge(pv_done, hd(1))
                    dve.wait_ge(silu_done, z_count)
                    nc.vector.tensor_tensor(aa[:, :], outp[:, 0:SEQ], heads(zslot)[:, b, :], ALU.mult).then_inc(aa_done, 1)
                if k == 14:
                    dve.wait_ge(a_hi_done, hd(1))
                    hi = a_hi[:, bass.ds(hd(0), 1), :].rearrange("p one t -> p (one t)").bitcast(F32)
                    nc.vector.tensor_tensor(a_lo[:, bass.ds(hd(0), 1), :].rearrange("p one t -> p (one t)"), aa[:, :], hi,
                                            ALU.subtract).then_inc(a_lo_done, 1)

            dve.wait_ge(sink_in, 16)
            dve.wait_ge(tab_in, 16)
            nc.vector.memset(eps_t[:, :], EPS).then_inc(eps_set, 1)
            dve.wait_ge(xsq, 4)
            sums = small[:, 0:4].rearrange("p (t half) -> p t half", half=2)
            nc.vector.tensor_reduce(small[:, 4:6], sums, AX_X, ALU.add).then_inc(xs_sum, 1)
            dve.wait_ge(xs_rs, 1)
            for t in range(TT):
                nc.vector.tensor_scalar(x_in[:, t, :], x_in[:, t, :], small[:, 8 + t:9 + t], None, ALU.mult).then_inc(x_scaled, 1)
            dve.wait_ge(vec_tr, 1)
            nc.vector.tensor_copy(vec[:, :], outp[:, 0:80]).then_inc(vec_ready, 1)
            spots = [lev[:, 0:512], lev[:, 512:1024], mis[:, :], outp[:, :]]
            for p in range(KT // 2):
                dve.wait_ge(h_hi_done, p + 1)
                for i in range(2):
                    kt = 2 * p + i
                    if p == 0 and i == 0:
                        dve.wait_ge(vec_ready, 1)
                    m = nc.vector.scalar_tensor_tensor(h_lo[:, kt, :], spots[p % 4][:, i * SEQ:(i + 1) * SEQ], vec[:, kt:kt + 1],
                                                       h_hi[:, kt, :].bitcast(F32), ALU.mult, ALU.subtract)
                m.then_inc(h_lo_done, 1)
            l0, l1 = vec[:, 32:48], vec[:, 48:64]
            dve.wait_ge(vec_ready, 1)
            nc.vector.tensor_tensor(lnm[:, 32:48], l0, l1, ALU.max).then_inc(lb_chain, 1)
            dve.wait_ge(lb_chain, 1)
            nc.vector.tensor_tensor(lnm[:, 0:16], l0, lnm[:, 32:48], ALU.subtract)
            nc.vector.tensor_tensor(lnm[:, 16:32], l1, lnm[:, 32:48], ALU.subtract).then_inc(lb_chain, 1)
            dve.wait_ge(lb_exp, 1)
            nc.vector.tensor_tensor(lnm[:, 48:64], lnm[:, 0:16], lnm[:, 16:32], ALU.add).then_inc(lb_chain, 1)
            dve.wait_ge(lb_chain, 3)
            nc.vector.reciprocal(lnm[:, 64:80], lnm[:, 48:64]).then_inc(lb_chain, 1)
            dve.wait_ge(lb_chain, 4)
            nc.vector.tensor_tensor(lb[:, :], lnm[:, 0:16], lnm[:, 64:80], ALU.mult).then_inc(lb_ready, 1)
            dve.wait_ge(lb_ready, 1)
            nc.vector.tensor_scalar(oml[:, :], lb[:, :], -1.0, 1.0, ALU.mult, ALU.add).then_inc(lb_ready, 1)

            def hgrn_group(n, e, hd, sil, slot, prev_slot, side, first=False):
                for b in range(4):
                    for k in range(KT):
                        rest_step(n, b * KT + k)
                        if not (first and b == 0):
                            pb = (b - 1) % 4
                            buf = flat((slot if b else prev_slot) + pb)
                            idx = e((-1, 0, 1, 1)[b])
                            if pb != 2:
                                sigmoid_parts(k, buf, idx, pb % 2, True if pb in (1, 3) else None)
                        if side:
                            hgrn_side(k, lambda i, b=b: hd(b + i), e(-2), sil(0), prev_slot, b)

            hgrn_group(count(0), count(0), None, count(0), 0, 4, False, first=True)
            with dve.Fori(1, GROUPS) as g:
                hgrn_group(count(0, 4 * KT, g), count(0, 3, g), count(-GH, GH, g), count(0, 2, g), (g % 2) * 4, ((g + 1) % 2) * 4, True)

            last_set = ((GROUPS - 1) % 2) * 4
            n = count(N_HG)
            for b in range(4):
                for k in range(KT):
                    rest_step(n, b * KT + k)
                    if b == 0:
                        sigmoid_parts(k, flat(last_set + 3), 3 * GROUPS - 1, 1, True)
                    hgrn_side(k, lambda i, b=b: (GROUPS - 1) * GH + b + i, 3 * GROUPS - 2, 2 * GROUPS, last_set, b)

            with dve.Fori(1, GROUPS) as g:
                n = count(N_KV, 2 * KT, g)
                hd = count(-GH, GH, g)
                for b in range(2):
                    for k in range(KT):
                        kk = b * KT + k
                        rest_step(n, kk)
                        if b == 0:
                            sigmoid_parts(k, flat(((g + 1) % 2) * 2 + 1), g + (3 * GROUPS - 1), 1, True)
                        attn_side(k % 16, lambda i, u=kk // 16: hd(u + i), g + 2 * GROUPS, ((g + 1) % 2) * 2 + 1, kk // 16)

            def merge(n, j, side):
                for k in range(N_GATE):
                    rest_step(n, k)
                    if side and k < 2 * KT:
                        zs = ((GROUPS - 1) % 2) * 2 + 1
                        if k < KT:
                            sigmoid_parts(k, flat(zs), 4 * GROUPS - 1, 1, True)
                        attn_side(k % 16, lambda i: (GROUPS - 1) * GH + k // 16 + i, 3 * GROUPS, zs, k // 16)
                    if k == 3 and not side:
                        add_b(j - 1, n(0))
                    if k == 2 * KT + UT + 3:
                        dve.wait_ge(pe_done, n(2 * KT + UT))
                        dve.wait_ge(sig_a_done, j + 1)
                        nc.vector.tensor_tensor(flat(j), flat(j), acc[:, 0, :], ALU.mult).then_inc(ya_done, 1)

            def add_b(j, n_end):
                dve.wait_ge(pe_done, n_end)
                dve.wait_ge(sig_b_done, j + 1)
                sb_flat = sig_b[:, :, :].rearrange("p h t -> p (h t)")
                nc.vector.tensor_tensor(sb_flat, sb_flat, acc[:, 1, :], ALU.mult).then_inc(yb_part, 1)
                dve.wait_ge(yb_part, j + 1)
                dve.wait_ge(ya_done, j + 1)
                nc.vector.tensor_tensor(flat(j), flat(j), sb_flat, ALU.add).then_inc(y_done, 1)

            merge(count(N_AT), 0, True)
            with dve.Fori(1, NB) as j:
                merge(count(N_AT, N_GATE, j), j, False)
            add_b(NB - 1, N_MERGE)

            def residual(i, par, n_end):
                dve.wait_ge(pe_done, n_end)
                cols = bass.ds(i * BLK, BLK)
                nc.vector.tensor_tensor(xr[:, :, cols], xr[:, :, cols], acc[:, par, :].rearrange("p (t n) -> p t n", t=TT), ALU.add
                                        ).then_inc(res_done, 1)

            def apply_gain(i):
                dve.wait_ge(rsq_done, i * 2 + 2)
                cols = bass.ds(i * BLK, BLK)
                gv = fgain[:, cols].unsqueeze(1).broadcast_to([P, TT, BLK])
                nc.vector.tensor_tensor(xr[:, :, cols], xr[:, :, cols], gv, ALU.mult).then_inc(gained, 1)

            def project(n, first, a):
                for b in range(2):
                    for k in range(KT):
                        if first and b == 0 and k % GH == 0:
                            j = k // GH
                            dve.wait_ge(y_hi_done, j + 1)
                            nc.vector.tensor_tensor(h_lo[:, j * GH:(j + 1) * GH, :], heads(j),
                                                    h_hi[:, j * GH:(j + 1) * GH, :].bitcast(F32), ALU.subtract).then_inc(y_lo_done, 1)
                        rest_step(n, b * KT + k)
                        if not (first and b == 0):
                            if k == 3:
                                if first:
                                    dve.wait_ge(xr_in, 16)
                                    dve.wait_ge(fgain_in, 16)
                                residual(a(b - 1), (b - 1) % 2, n(b * KT))
                            if k == 9:
                                apply_gain(a(b - 1))

            project(count(N_MERGE), True, count(0))
            with dve.Fori(1, NB // 2) as m:
                project(count(N_MERGE, 2 * KT, m), False, count(0, 2, m))
            residual(NB - 1, 1, N_MERGE + NB * KT)
            dve.wait_ge(rsq_done, 2 * NB)
            nc.vector.tensor_reduce(small[:, 0:2], ssq[:, :, :], AX_X, ALU.add).then_inc(fs_sum, 1)
            apply_gain(NB - 1)
            dve.wait_ge(gained, NB)
            dve.wait_ge(fs_rs, 1)
            for i in range(4):
                cols = slice(i * (D // 4), (i + 1) * (D // 4))
                nc.vector.tensor_scalar(xr[:, 0, cols], xr[:, 0, cols], small[:, 4:5], None, ALU.mult).then_inc(fin_v, 1)


_INS = ["x", "norm_gain", "w_in", "attn_sinks", "lb_logits", "hgrn_norm_gain", "w_up_attn", "w_up_hgrn",
        "w_out", "final_norm_gain"]


def constant_tables(np):
    tab = np.zeros((P, T_ALL), np.float32)
    i = np.arange(P)
    s, t = i[:, None], i[None, :]
    for n, m in enumerate(HALVES):
        own = (s // (2 * m) == t // (2 * m)) & (s % (2 * m) < m) & (t % (2 * m) >= m)
        tab[:, T_LEV + n * P:T_LEV + (n + 1) * P] = own
    tab[:, T_LEV + NL * P:T_LEV + (NL + 1) * P] = s == t
    for tile in range(TT):
        first = T_AM + tile * P
        width = P * (tile + 1)
        tc = (tile * P + i[:, None]) // CHUNK
        sc = np.arange(width)[None, :] // CHUNK
        tab[:, first:first + width] = np.where((sc == tc) | (sc == tc - 1), 0.0, -3e38)
    tab[:, T_SCAN:T_SCAN + SEQ] = np.arange(SEQ) % CHUNK != 0
    tab[:, T_ID:T_ID + P] = s == t
    tab[:, T_MEAN:T_MEAN + P] = 1.0 / HD
    return tab


def kernel(**inputs):
    import numpy as _np
    import concourse.bacc as _bacc
    from concourse import mybir as _mybir
    from concourse.bass_utils import run_bass_kernel_spmd as _run

    nc = _bacc.Bacc("TRN2", target_bir_lowering=False, num_devices=1)
    arrays, args = {}, []
    for name in _INS:
        a = _np.ascontiguousarray(inputs[name])
        arrays[f"in_{name}_dram"] = a
        args.append(nc.dram_tensor(f"in_{name}_dram", a.shape, _mybir.dt.from_np(a.dtype), kind="ExternalInput").ap())
    arrays["tables_dram"] = constant_tables(_np)
    args.append(nc.dram_tensor("tables_dram", (P, T_ALL), _mybir.dt.float32, kind="ExternalInput").ap())
    args.append(nc.dram_tensor("out_0_dram", (1, SEQ, D), _mybir.dt.float32, kind="ExternalOutput").ap())
    build(nc, *args)
    r = _run(nc, [arrays], core_ids=[0])
    return r.results[0]["out_0_dram"]
```

```python
from contextlib import ExitStack

import concourse.bass as bass
from concourse import mybir

P = 128
F32 = mybir.dt.float32
F32R = mybir.dt.float32r
ALU = mybir.AluOpType
ACT = mybir.ActivationFunctionType
AX_X = mybir.AxisListType.X

SEQ = 256
TT = SEQ // P
D = 4096
KT = D // P
HD = 128
HEADS = 16
KVH = 4
GH = 4
GROUPS = HEADS // GH
CHUNK = 64
CHUNKS = SEQ // CHUNK
BLK = GH * HD
WID = HEADS * HD
UT = WID // P
NB = D // BLK
EPS = 1e-6
SCALE = float(HD) ** -0.5

C_QA, C_KA, C_VA, C_ZA = 0, WID, WID + KVH * HD, WID + 2 * KVH * HD
C_QB = C_ZA + WID
C_FB, C_IB, C_ZB = C_QB + WID, C_QB + 2 * WID, C_QB + 3 * WID
C_GA = C_ZB + WID
C_GB = C_GA + D

HALVES = [CHUNK // 2 >> i for i in range(6)]
NL = len(HALVES)
L_G, L_END = NL, NL + 1

T_LEV = 0
T_AM = T_LEV + (NL + 1) * P
T_SCAN = T_AM + P + SEQ
T_ID = T_SCAN + SEQ
T_MEAN = T_ID + P
T_ALL = T_MEAN + P

RING = 4

N_HG = GROUPS * 4 * KT
N_KV = N_HG + 2 * KT
N_AT = N_KV + GROUPS * 2 * KT
N_GATE = 2 * KT + 2 * UT
N_MERGE = N_AT + NB * N_GATE


Y_AT = [0, 2] + [GH * (j - 1) for j in range(2, NB)]


def count(base, per=0, it=0):
    def c(k=0, unit=1):
        if isinstance(it, int):
            return (base + per * it + k) // unit
        assert per % unit == 0
        return it * (per // unit) + (base + k) // unit
    return c


def build(nc, x, norm_gain, w_in, attn_sinks, lb_logits, hgrn_norm_gain, w_up_attn, w_up_hgrn,
          w_out, final_norm_gain, tables, out):
    ctx = ExitStack()
    with ctx:
        def sb(name, shape, dt=F32):
            return ctx.enter_context(nc.sbuf_tensor(name, shape, dt))

        def sem(name):
            return ctx.enter_context(nc.semaphore(name))

        raw = sb("raw", [P, RING, 2, BLK])
        w_hi = sb("w_hi", [P, RING, BLK], F32R)
        w_lo = sb("w_lo", [P, RING, BLK], F32R)
        h_hi = sb("h_hi", [P, KT, SEQ], F32R)
        h_lo = sb("h_lo", [P, KT, SEQ], F32R)
        region_base = nc.sbuf_base
        sb("branch_region", [P, 4 * UT * SEQ])
        proj_base = nc.sbuf_base
        sb("proj_region", [P, NB * GH * SEQ])
        k_att = sb("k_att", [P, GH, SEQ])
        v_att = sb("v_att", [P, TT, BLK])
        tab = sb("tab", [P, T_ALL])
        vec = sb("vec", [P, 80])
        lb = sb("lb", [P, HEADS])
        oml = sb("oml", [P, HEADS])
        sink = sb("sink", [P, HEADS])
        ssq = sb("ssq", [P, TT, NB])
        small = sb("small", [P, 16])
        eps_t = sb("eps_t", [P, 1])

        def at(base, name, shape, dt=F32):
            n = 4
            for s in shape[1:]:
                n *= s
            return nc.alloc_sbuf_tensor_at(name, shape, dt, offset=base), base + n

        a_hi, b1 = at(region_base, "a_hi", [P, UT, SEQ], F32R)
        a_lo, b2 = at(b1, "a_lo", [P, UT, SEQ], F32R)
        b_hi, b3 = at(b2, "b_hi", [P, UT, SEQ], F32R)
        b_lo, _ = at(b3, "b_lo", [P, UT, SEQ], F32R)
        decay, q = at(region_base, "decay", [P, NL + 2, SEQ])
        lev_m, q = at(q, "lev_m", [P, NL + 1, P])
        at_m, q = at(q, "at_m", [P, TT, P])
        fg, q = at(q, "fg", [P, SEQ])
        kf, q = at(q, "kf", [P, SEQ])
        gl, q = at(q, "gl", [P, SEQ])
        qg, q = at(q, "qg", [P, SEQ])
        kd_t, q = at(q, "kd_t", [P, TT, HD])
        iv, q = at(q, "iv", [P, TT, HD])
        state, q = at(q, "state", [P, CHUNKS - 1, HD])
        osq, q = at(q, "osq", [P, SEQ])
        rs, q = at(q, "rs", [P, SEQ])
        bb1, q = at(q, "bb1", [P, SEQ])
        bb2, q = at(q, "bb2", [P, SEQ])
        assert q <= b2
        x_in, q = at(region_base, "x_in", [P, TT, D])
        vrow, q = at(q, "vrow", [80, P])
        lbw, q = at(q, "lbw", [P, 80])
        xr, q = at(region_base, "xr", [P, TT, D])
        fgain, q = at(q, "fgain", [P, D])
        sq_o, q = at(q, "sq_o", [P, BLK])
        proj, _ = at(proj_base, "proj", [P, NB, GH * SEQ])
        sq_x, _ = at(proj_base, "sq_x", [P, D // 2])
        q = proj_base + 4 * 4 * GH * SEQ
        s_sb, q = at(q, "s_sb", [P, P + SEQ])
        p_t, q = at(q, "p_t", [P, 3, P])
        qw, q = at(q, "qw", [P, SEQ])
        vw, q = at(q, "vw", [P, TT, HD])
        aa, q = at(q, "aa", [P, SEQ])
        mx, q = at(q, "mx", [P, 8])
        negm, q = at(q, "negm", [P, 8])
        rowsum, q = at(q, "rowsum", [P, 8])
        esink, q = at(q, "esink", [P, 8])
        den, q = at(q, "den", [P, 8])
        rden, q = at(q, "rden", [P, 8])
        sig_b = k_att

        acc = ctx.enter_context(nc.psum_tensor("acc", [P, 2, 2 * BLK], F32))
        lev = ctx.enter_context(nc.psum_tensor("lev", [P, 2 * 512], F32))
        mis = ctx.enter_context(nc.psum_tensor("mis", [P, 512], F32))
        outp = ctx.enter_context(nc.psum_tensor("outp", [P, 512], F32))

        w_landed = [sem(f"w_landed{i}") for i in range(RING)]
        hi_ready = sem("hi_ready")
        lo_ready = sem("lo_ready")
        pe_done = sem("pe_done")
        tab_in, vec_in, sink_in = sem("tab_in"), sem("vec_in"), sem("sink_in")
        x_landed = [sem(f"x_landed{i}") for i in range(4)]
        eps_set = sem("eps_set")
        xsq = sem("xsq")
        xs_sum, xs_root, xs_rs, x_scaled = sem("xs_sum"), sem("xs_root"), sem("xs_rs"), sem("x_scaled")
        x_tr, h_hi_done, h_lo_done = sem("x_tr"), sem("h_hi_done"), sem("h_lo_done")
        vec_tr, vec_ready = sem("vec_tr"), sem("vec_ready")
        lb_chain, lb_exp, lb_ready = sem("lb_chain"), sem("lb_exp"), sem("lb_ready")
        sig_f_done = sem("sig_f_done")
        silu_done, i_copied, kv_copied, qa_copied = sem("silu_done"), sem("i_copied"), sem("kv_copied"), sem("qa_copied")
        fg_done, kf_done, ln_done, g_done = sem("fg_done"), sem("kf_done"), sem("ln_done"), sem("g_done")
        dec_args, dec_done, dec_mul, iv_done = sem("dec_args"), sem("dec_done"), sem("dec_mul"), sem("iv_done")
        kd_tr, kd_copied, levels_done = sem("kd_tr"), sem("kd_copied"), sem("levels_done")
        masked, att_done, kv_done = sem("masked"), sem("att_done"), sem("kv_done")
        st_done = [sem(f"st_done{i}") for i in range(CHUNKS - 1)]
        ho_done, osq_done, mean_done, root_done, rs_done = sem("ho_done"), sem("osq_done"), sem("mean_done"), sem("root_done"), sem("rs_done")
        bb1_done, bb2_done, b_hi_done, b_lo_done = sem("bb1_done"), sem("bb2_done"), sem("b_hi_done"), sem("b_lo_done")
        qvw_done, score_done, s_masked, mx_done, negm_done = sem("qvw_done"), sem("score_done"), sem("s_masked"), sem("mx_done"), sem("negm_done")
        p_exp, den_done, rden_done, p_norm = sem("p_exp"), sem("den_done"), sem("rden_done"), sem("p_norm")
        p_tr, pt_copied, pv_done, aa_done, a_hi_done, a_lo_done = sem("p_tr"), sem("pt_copied"), sem("pv_done"), sem("aa_done"), sem("a_hi_done"), sem("a_lo_done")
        sig_a_done, sig_b_done, ya_done, yb_part, y_done = sem("sig_a_done"), sem("sig_b_done"), sem("ya_done"), sem("yb_part"), sem("y_done")
        y_hi_done, y_lo_done = sem("y_hi_done"), sem("y_lo_done")
        xr_in = [sem("xr_in0"), sem("xr_in1")]
        res_done, rsq_done, gained = sem("res_done"), sem("rsq_done"), sem("gained")
        fs_sum, fs_root, fs_rs, fin_v, fin_s, stored = sem("fs_sum"), sem("fs_root"), sem("fs_rs"), sem("fin_v"), sem("fin_s"), sem("stored")

        ident = tab[:, T_ID:T_ID + P]
        x_rows = x.rearrange("b (t p) d -> p (b t) d", p=P)
        out_rows = out.rearrange("b (t p) d -> p (b t) d", p=P)
        w_in_r = w_in.rearrange("l (c p) n -> p (l c) n", p=P)
        w_ua_r = w_up_attn.rearrange("l (c p) n -> p (l c) n", p=P)
        w_uh_r = w_up_hgrn.rearrange("l (c p) n -> p (l c) n", p=P)
        w_out_r = w_out.rearrange("l (c p) n -> p (l c) n", p=P)
        g_view = decay[:, L_G, :]
        spots = [lev[:, 0:512], lev[:, 512:1024], mis[:, :], outp[:, :]]
        kv_spot = [mis[:, 0:HD], outp[:, SEQ:SEQ + HD], mis[:, HD:2 * HD]]

        def heads(slot):
            return proj[:, bass.ds(slot, 1), :].rearrange("p one (h t) -> p (one h) t", h=GH)

        def flat(slot):
            return proj[:, bass.ds(slot, 1), :].rearrange("p one n -> p (one n)")

        def rows(slot):
            return proj[:, bass.ds(slot, 1), :].rearrange("p one (t n) -> p (one t) n", t=TT)

        block = ctx.enter_context(nc.Block())

        @block.sync
        def _(sp):
            for t in range(TT):
                for half in range(2):
                    cols = slice(half * (D // 2), (half + 1) * (D // 2))
                    sp.dma_start(x_in[:, t, cols], x_rows[:, t, cols]).then_inc(x_landed[2 * t + half], 16)
                if t == 0:
                    sp.dma_start(vrow[0:32, :], norm_gain.rearrange("a (c p) -> (a c) p", p=P)).then_inc(vec_in, 16)
                    sp.dma_start(vrow[32:64, :], lb_logits.rearrange("a (c p) -> (a c) p", p=P)).then_inc(vec_in, 16)
                    sp.dma_start(vrow[64:80, :], hgrn_norm_gain.rearrange("a (c p) -> (a c) p", p=P)).then_inc(vec_in, 16)
                    sp.dma_start(sink[:, :], attn_sinks.broadcast_to([P, HEADS])).then_inc(sink_in, 16)
                    sp.dma_start(tab[:, :], tables).then_inc(tab_in, 16)

            def load_steps(n, w, col, steps, first=0):
                with sp.Fori(0, steps // (2 * RING)) as c:
                    for r in range(RING):
                        sp.wait_ge(lo_ready, c * (2 * RING) + n(2 * r - 2 * RING + 2))
                        sp.dma_start(raw[:, r, :, :], w[:, bass.ds(c * (2 * RING) + (first + 2 * r), 2), bass.ds(col, BLK)]
                                     ).then_inc(w_landed[r], 16)

            def load_first(w, col):
                for r in range(RING):
                    sp.dma_start(raw[:, r, :, :], w[:, 2 * r:2 * r + 2, bass.ds(col, BLK)]).then_inc(w_landed[r], 16)
                with sp.Fori(1, KT // (2 * RING)) as c:
                    for r in range(RING):
                        sp.wait_ge(lo_ready, c * (2 * RING) + (2 * r - 2 * RING + 2))
                        sp.dma_start(raw[:, r, :, :], w[:, bass.ds(c * (2 * RING) + 2 * r, 2), bass.ds(col, BLK)]
                                     ).then_inc(w_landed[r], 16)

            load_first(w_in_r, C_FB)
            for b, c0 in ((1, C_QB), (2, C_IB), (3, C_ZB)):
                load_steps(count(b * KT), w_in_r, c0, KT)
            with sp.Fori(1, GROUPS) as g:
                for b, c0 in enumerate((C_FB, C_QB, C_IB, C_ZB)):
                    load_steps(count(b * KT, 4 * KT, g), w_in_r, g * BLK + c0, KT)
            load_steps(count(N_HG), w_in_r, C_KA, KT)
            load_steps(count(N_HG + KT), w_in_r, C_VA, KT)
            with sp.Fori(0, GROUPS) as g:
                for b, c0 in enumerate((C_QA, C_ZA)):
                    load_steps(count(N_KV + b * KT, 2 * KT, g), w_in_r, g * BLK + c0, KT)
            with sp.Fori(0, NB) as j:
                load_steps(count(N_AT, N_GATE, j), w_in_r, j * BLK + C_GA, KT)
                load_steps(count(N_AT + KT, N_GATE, j), w_in_r, j * BLK + C_GB, KT)
                load_steps(count(N_AT + 2 * KT, N_GATE, j), w_ua_r, j * BLK, UT)
                load_steps(count(N_AT + 2 * KT + UT, N_GATE, j), w_uh_r, j * BLK, UT)
            fgain_rows = final_norm_gain.rearrange("(a d) -> a d", a=1).broadcast_to([P, D])

            def load_tail(n, par):
                cols = bass.ds(n * BLK, BLK)
                sp.dma_start(xr[:, :, cols], x_rows[:, :, cols]).then_inc(xr_in[par], 16)
                sp.dma_start(fgain[:, cols], fgain_rows[:, cols]).then_inc(xr_in[par], 16)

            load_steps(count(N_MERGE), w_out_r, 0, KT // 2)
            sp.wait_ge(pe_done, N_MERGE)
            load_tail(0, 0)
            load_steps(count(N_MERGE + KT // 2), w_out_r, 0, KT // 2, first=KT // 2)
            load_tail(1, 1)
            load_steps(count(N_MERGE + KT), w_out_r, BLK, KT)
            with sp.Fori(1, NB // 2) as m:
                for b in range(2):
                    load_tail(m * 2 + b, b)
                    load_steps(count(N_MERGE + b * KT, 2 * KT, m), w_out_r, m * (2 * BLK) + b * BLK, KT)
            for i in range(4):
                cols = slice(i * (D // 4), (i + 1) * (D // 4))
                sp.wait_ge(fin_v, i + 1)
                sp.dma_start(out_rows[:, 0, cols], xr[:, 0, cols]).then_inc(stored, 16)
                sp.wait_ge(fin_s, i + 1)
                sp.dma_start(out_rows[:, 1, cols], xr[:, 1, cols]).then_inc(stored, 16)
            sp.wait_ge(stored, 8 * 16)

        @block.tensor
        def _(pe):
            def step_t(n, k, par, r_hi, r_lo, kt, last, free):
                s = k % RING
                if kt == 0 and free is not None:
                    pe.wait_ge(*free)
                pe.wait_ge(lo_ready, n(k + 1))
                for c in range(GH):
                    o = acc[:, par, c * SEQ:(c + 1) * SEQ]
                    cols = slice(c * HD, (c + 1) * HD)
                    first = kt == 0 and c % 2 == 0
                    nc.tensor.matmul(o, w_hi[:, s, cols], r_hi[:, kt, :], start=first, stop=False)
                    nc.tensor.matmul(o, w_hi[:, s, cols], r_lo[:, kt, :], start=False, stop=False)
                    m = nc.tensor.matmul(o, w_lo[:, s, cols], r_hi[:, kt, :], start=False, stop=last and c % 2 == 1)
                m.then_inc(pe_done, 1)

            def step_r(n, k, par, kt, last, free):
                s = k % RING
                if kt == 0 and free is not None:
                    pe.wait_ge(*free)
                pe.wait_ge(lo_ready, n(k + 1))
                for t in range(TT):
                    o = acc[:, par, t * BLK:(t + 1) * BLK]
                    tok = slice(t * P, (t + 1) * P)
                    nc.tensor.matmul(o, h_hi[:, kt, tok], w_hi[:, s, :], start=kt == 0, stop=False)
                    nc.tensor.matmul(o, h_lo[:, kt, tok], w_hi[:, s, :], start=False, stop=False)
                    m = nc.tensor.matmul(o, h_hi[:, kt, tok], w_lo[:, s, :], start=False, stop=last)
                m.then_inc(pe_done, 1)

            def levels(t, head):
                tok = slice(t * P, (t + 1) * P)
                for i in range(NL):
                    nc.tensor.matmul(lev[:, i * P:(i + 1) * P], decay[:, i, tok], decay[:, i, tok], start=True, stop=True)
                return tok

            def hgrn_side(k, hd, slot, b):
                if k == 12:
                    pe.wait_ge(dec_mul, hd(1))
                    for t in range(TT):
                        m = nc.tensor.transpose(mis[:, t * P:(t + 1) * P], decay[:, L_END, t * P:(t + 1) * P], ident)
                    m.then_inc(kd_tr, 1)
                if k == 12 or k == 17:
                    t = (k - 12) // 5
                    if t:
                        pe.wait_ge(masked, hd(0) * 2 + 1)
                    tok = levels(t, hd)
                    nc.tensor.matmul(lev[:, NL * P:(NL + 1) * P], kf[:, tok], heads(slot + 1)[:, b, tok],
                                     start=True, stop=True).then_inc(levels_done, 1)
                if k == 17:
                    pe.wait_ge(kd_copied, hd(1))
                    pe.wait_ge(iv_done, hd(1))
                    for c in range(CHUNKS - 1):
                        part = slice((c % 2) * CHUNK, (c % 2 + 1) * CHUNK)
                        m = nc.tensor.matmul(kv_spot[c], kd_t[part, c // 2, :], iv[part, c // 2, :],
                                             start=True, stop=True)
                    m.then_inc(kv_done, 1)
                if k == 23:
                    pe.wait_ge(att_done, hd(0) * 2 + 2)
                    pe.wait_ge(st_done[-1], hd(1))
                    for t in range(TT):
                        nc.tensor.matmul(outp[:, t * P:(t + 1) * P], iv[:, t, :], at_m[:, t, :], start=True, stop=False)
                        for c in range(max(1, 2 * t), 2 * t + 2):
                            cols = slice(c * CHUNK, (c + 1) * CHUNK)
                            m = nc.tensor.matmul(outp[:, cols], state[:, c - 1, :], qg[:, cols],
                                                 start=False, stop=c == 2 * t + 1)
                    m.then_inc(ho_done, 1)
                if k == 27:
                    pe.wait_ge(osq_done, hd(1))
                    nc.tensor.matmul(outp[:, SEQ:2 * SEQ], tab[:, T_MEAN:T_MEAN + P], osq[:, :],
                                     start=True, stop=True).then_inc(mean_done, 1)

            def attn_side(k, hd, g):
                if k == 1:
                    pe.wait_ge(qvw_done, hd(1))
                    keys = k_att[:, bass.ds(g, 1), :].rearrange("p one t -> p (one t)")
                    nc.tensor.matmul(lev[:, 0:P], qw[:, 0:P], keys[:, 0:P], start=True, stop=True)
                    nc.tensor.matmul(lev[:, P:P + SEQ], qw[:, P:SEQ], keys, start=True, stop=True).then_inc(score_done, 1)
                if k == 6:
                    pe.wait_ge(p_norm, hd(1))
                    for i in range(3):
                        m = nc.tensor.transpose(mis[:, i * P:(i + 1) * P], s_sb[:, i * P:(i + 1) * P], ident)
                    m.then_inc(p_tr, 1)
                if k == 10:
                    pe.wait_ge(pt_copied, hd(1))
                    nc.tensor.matmul(outp[:, 0:P], vw[:, 0, :], p_t[:, 0, :], start=True, stop=True)
                    nc.tensor.matmul(outp[:, P:SEQ], vw[:, 0, :], p_t[:, 1, :], start=True, stop=False)
                    nc.tensor.matmul(outp[:, P:SEQ], vw[:, 1, :], p_t[:, 2, :], start=False, stop=True).then_inc(pv_done, 1)

            pe.wait_ge(vec_in, 48)
            pe.wait_ge(tab_in, 16)
            nc.tensor.transpose(outp[:, 0:80], vrow[0:80, :], ident[0:80, 0:80]).then_inc(vec_tr, 1)
            def input_pair(p):
                if p % 4 == 0:
                    pe.wait_ge(x_scaled, TT * (p // 4 + 1))
                if p == 3:
                    pe.wait_ge(vec_ready, 1)
                if p >= 4:
                    pe.wait_ge(h_lo_done, p - 3)
                for i in range(2):
                    for t in range(TT):
                        kt = 2 * p + i
                        m = nc.tensor.transpose(spots[p % 4][:, (i * TT + t) * P:(i * TT + t + 1) * P],
                                                x_in[:, t, kt * P:(kt + 1) * P], ident)
                m.then_inc(x_tr, 1)

            def hgrn_group(n, g, hd, slot, side):
                before = [(i_copied, g), (silu_done, g * 2), (sig_f_done, g + 1), (silu_done, g * 2 + 1)]
                for b in range(4):
                    free = before[b] if side or b >= 2 else None
                    for k in range(KT):
                        kk = b * KT + k
                        if not side and b == 0 and k % 2 == 0:
                            pe.wait_ge(h_lo_done, k // 2 + 1)
                        if b == 2:
                            step_r(n, kk, b % 2, k, k == KT - 1, free)
                        else:
                            step_t(n, kk, b % 2, h_hi, h_lo, k, k == KT - 1, free)
                        if side:
                            hgrn_side(k, lambda i, b=b: hd(b + i), slot, b)
                        elif b == 0 and k % 2 == 0 and k // 2 + 3 < KT // 2:
                            input_pair(k // 2 + 3)

            for p in range(3):
                input_pair(p)
            hgrn_group(count(0), 0, None, None, False)
            with pe.Fori(1, GROUPS) as g:
                hgrn_group(count(0, 4 * KT, g), g, count(-GH, GH, g), ((g + 1) % 2) * 4, True)

            last_set = ((GROUPS - 1) % 2) * 4
            n = count(N_HG)
            before = [(i_copied, GROUPS), (silu_done, 2 * GROUPS), (kv_copied, 1), (kv_copied, 2)]
            for b in range(4):
                for k in range(KT):
                    kk = b * KT + k
                    free = before[b]
                    if b == 1:
                        step_r(n, kk, b % 2, k, k == KT - 1, free)
                    else:
                        step_t(n, kk, b % 2, h_hi, h_lo, k, k == KT - 1, free)
                    hgrn_side(k, lambda i, b=b: (GROUPS - 1) * GH + b + i, last_set, b)

            def attn_blocks(n, hd, g):
                before = [(qa_copied, g + 1), (silu_done, g + (2 * GROUPS + 1))]
                for b in range(2):
                    for k in range(KT):
                        kk = b * KT + k
                        step_t(n, kk, b % 2, h_hi, h_lo, k, k == KT - 1, before[b])
                        attn_side(k % 16, lambda i, u=kk // 16: hd(u + i), g)

            with pe.Fori(1, GROUPS) as g:
                attn_blocks(count(N_KV, 2 * KT, g), count(-GH, GH, g), g - 1)

            def merge(n, j, side):
                before = [(qa_copied, GROUPS), (silu_done, 3 * GROUPS)] if side else [(ya_done, j), (yb_part, j)]
                for k in range(2 * KT):
                    step_t(n, k, k // KT, h_hi, h_lo, k % KT, k % KT == KT - 1, before[k // KT])
                    if side:
                        attn_side(k % 16, lambda i, u=k // 16: (GROUPS - 1) * GH + u + i, GROUPS - 1)
                if side:
                    pe.wait_ge(a_lo_done, HEADS)
                    pe.wait_ge(b_lo_done, HEADS)
                for k in range(UT):
                    step_t(n, 2 * KT + k, 0, a_hi, a_lo, k, k == UT - 1, (sig_a_done, j + 1))
                for k in range(UT):
                    step_t(n, 2 * KT + UT + k, 1, b_hi, b_lo, k, k == UT - 1, (sig_b_done, j + 1))

            merge(count(N_AT), 0, True)
            with pe.Fori(1, NB) as j:
                merge(count(N_AT, N_GATE, j), j, False)

            def project(n, before, first):
                for b in range(2):
                    for k in range(KT):
                        if first and b == 0 and k % GH == 0:
                            pe.wait_ge(y_lo_done, k // GH + 1)
                        step_r(n, b * KT + k, b, k, k == KT - 1, before[b])

            project(count(N_MERGE), [(ya_done, NB), (yb_part, NB)], True)
            with pe.Fori(1, NB // 2) as m:
                project(count(N_MERGE, 2 * KT, m), [(res_done, m * 2 - 1), (res_done, m * 2)], False)

        @block.scalar
        def _(act):
            def round_step(n, k, fresh=False):
                if k % 2 == 0:
                    act.wait_ge(w_landed[(k // 2) % RING], (n(k, 2 * RING) + 1) * 16)
                if not (fresh and k < RING):
                    act.wait_ge(pe_done, n(k - RING + 1))
                nc.scalar.activation(w_hi[:, k % RING, :], raw[:, (k // 2) % RING, k % 2, :], ACT.Copy).then_inc(hi_ready, 1)

            def silu(dst, par, n_end):
                act.wait_ge(pe_done, n_end)
                nc.scalar.activation(dst, acc[:, par, :], ACT.Silu).then_inc(silu_done, 1)

            def hgrn_epilogue(b, par, n_end, slot):
                if b == 2:
                    act.wait_ge(pe_done, n_end)
                    nc.scalar.activation(flat(slot + 2), acc[:, par, :], ACT.Copy).then_inc(i_copied, 1)
                elif b == 0:
                    act.wait_ge(pe_done, n_end)
                    nc.scalar.activation(flat(slot), acc[:, par, :], ACT.Sigmoid).then_inc(sig_f_done, 1)
                else:
                    silu(flat(slot + b), par, n_end)

            def hgrn_side(k, hd, g1, slot, b):
                if k == 9:
                    if b == 0:
                        act.wait_ge(i_copied, g1)
                    nc.scalar.activation(iv[:, :, :], rows(slot + 2)[:, :, b * HD:(b + 1) * HD], ACT.Copy).then_inc(iv_done, 1)
                if k == 1:
                    act.wait_ge(fg_done, hd(1))
                    nc.scalar.activation(gl[:, :], fg[:, :], ACT.Ln).then_inc(ln_done, 1)
                if k in (6, 7):
                    act.wait_ge(dec_args, hd(1))
                    part = decay[:, (k - 6) * 4:(k - 5) * 4, :]
                    nc.scalar.activation(part, part, ACT.Exp).then_inc(dec_done, 1)
                if k == 15:
                    act.wait_ge(kd_tr, hd(1))
                    nc.scalar.activation(kd_t[:, :, :], mis[:, 0:TT * P].rearrange("p (t d) -> p t d", t=TT), ACT.Copy
                                         ).then_inc(kd_copied, 1)
                if k == 25:
                    act.wait_ge(ho_done, hd(1))
                    nc.scalar.activation(osq[:, :], outp[:, 0:SEQ], ACT.Square).then_inc(osq_done, 1)
                if k == 29:
                    act.wait_ge(mean_done, hd(1))
                    nc.scalar.activation(rs[:, :], outp[:, SEQ:2 * SEQ], ACT.Sqrt, bias=eps_t[:, :]).then_inc(root_done, 1)
                if k == 31:
                    act.wait_ge(bb2_done, hd(1))
                    nc.scalar.activation(b_hi[:, bass.ds(hd(0), 1), :].rearrange("p one t -> p (one t)"), bb2[:, :], ACT.Copy
                                         ).then_inc(b_hi_done, 1)

            def attn_side(k, hd, g):
                if k == 4:
                    act.wait_ge(negm_done, hd(1))
                    cuts = (slice(0, P), slice(P, P + SEQ))
                    for t in range(TT):
                        nc.scalar.activation(s_sb[:, cuts[t]], s_sb[:, cuts[t]], ACT.Exp, bias=negm[:, t:t + 1],
                                             accum_out=rowsum[:, t:t + 1])
                    nc.scalar.activation(esink[:, 0:TT], negm[:, 0:TT], ACT.Exp, bias=sink[:, bass.ds(hd(0), 1)]).then_inc(p_exp, 1)
                if k == 9:
                    act.wait_ge(p_tr, hd(1))
                    nc.scalar.activation(p_t[:, :, :], mis[:, 0:3 * P].rearrange("p (i t) -> p i t", i=3), ACT.Copy).then_inc(pt_copied, 1)
                if k == 14:
                    act.wait_ge(aa_done, hd(1))
                    nc.scalar.activation(a_hi[:, bass.ds(hd(0), 1), :].rearrange("p one t -> p (one t)"), aa[:, :], ACT.Copy
                                         ).then_inc(a_hi_done, 1)

            def attn_load(k, hd, g, qslot, b):
                if k == 0:
                    act.wait_ge(qa_copied, g + 1)
                    act.wait_ge(kv_copied, 2)
                    nc.scalar.activation(qw[:, :], heads(qslot)[:, b, :], ACT.Copy, scale=SCALE)
                    nc.scalar.activation(vw[:, :, :], v_att[:, :, bass.ds(g * HD, HD)], ACT.Copy).then_inc(qvw_done, 1)

            act.wait_ge(sink_in, 16)
            for i in range(4):
                act.wait_ge(x_landed[i], 16)
                if i:
                    act.wait_ge(xsq, i)
                nc.scalar.activation(sq_x[:, :], x_in[:, i // 2, (i % 2) * (D // 2):(i % 2 + 1) * (D // 2)], ACT.Square,
                                     accum_out=small[:, i:i + 1]).then_inc(xsq, 1)
            act.wait_ge(xs_sum, 1)
            act.wait_ge(eps_set, 1)
            nc.scalar.activation(small[:, 6:8], small[:, 4:6], ACT.Sqrt, scale=1.0 / D, bias=eps_t[:, :]).then_inc(xs_root, 1)
            act.wait_ge(vec_ready, 1)

            def input_pair(p):
                act.wait_ge(x_tr, p + 1)
                for i in range(2):
                    kt = 2 * p + i
                    m = nc.scalar.activation(h_hi[:, kt, :], spots[p % 4][:, i * SEQ:(i + 1) * SEQ], ACT.Copy, scale=vec[:, kt:kt + 1])
                m.then_inc(h_hi_done, 1)
            act.wait_ge(lb_chain, 2)
            nc.scalar.activation(lbw[:, 0:32], lbw[:, 0:32], ACT.Exp).then_inc(lb_exp, 1)
            input_pair(0)

            def hgrn_group(n, hd, g, slot, prev_slot, side, first=False):
                for b in range(4):
                    for k in range(KT):
                        kk = b * KT + k
                        if first and b == 0 and k % 2 == 0 and k // 2 + 1 < KT // 2:
                            input_pair(k // 2 + 1)
                        round_step(n, kk, fresh=first and b == 0)
                        if k == 3 and not (first and b == 0):
                            pb = (b - 1) % 4
                            hgrn_epilogue(pb, pb % 2, n(b * KT), slot if b else prev_slot)
                        if side:
                            hgrn_side(k, lambda i, b=b: hd(b + i), g, prev_slot, b)

            hgrn_group(count(0), None, 0, 0, 4, False, first=True)
            with act.Fori(1, GROUPS) as g:
                hgrn_group(count(0, 4 * KT, g), count(-GH, GH, g), g, (g % 2) * 4, ((g + 1) % 2) * 4, True)

            last_set = ((GROUPS - 1) % 2) * 4
            n = count(N_HG)
            for b in range(4):
                for k in range(KT):
                    round_step(n, b * KT + k)
                    if k == 3:
                        if b == 0:
                            hgrn_epilogue(3, 1, n(0), last_set)
                        elif b == 1:
                            act.wait_ge(pe_done, n(KT))
                            nc.scalar.activation(k_att[:, :, :], acc[:, 0, :].rearrange("p (h t) -> p h t", h=GH), ACT.Copy).then_inc(kv_copied, 1)
                        elif b == 2:
                            act.wait_ge(pe_done, n(2 * KT))
                            nc.scalar.activation(v_att[:, :, :], acc[:, 1, :].rearrange("p (t c) -> p t c", t=TT), ACT.Copy).then_inc(kv_copied, 1)
                        else:
                            act.wait_ge(pe_done, n(3 * KT))
                            nc.scalar.activation(flat(0), acc[:, 0, :], ACT.Copy).then_inc(qa_copied, 1)
                    hgrn_side(k, lambda i, b=b: (GROUPS - 1) * GH + b + i, GROUPS, last_set, b)

            with act.Fori(1, GROUPS) as g:
                n = count(N_KV, 2 * KT, g)
                hd = count(-GH, GH, g)
                for b in range(2):
                    for k in range(KT):
                        kk = b * KT + k
                        round_step(n, kk)
                        attn_load(k % 16, lambda i, u=kk // 16: hd(u + i), g - 1, ((g + 1) % 2) * 2, kk // 16)
                        if k == 3 and b == 0:
                            silu(flat(((g + 1) % 2) * 2 + 1), 1, n(0))
                        if k == 3 and b == 1:
                            act.wait_ge(pe_done, n(KT))
                            nc.scalar.activation(flat((g % 2) * 2), acc[:, 0, :], ACT.Copy).then_inc(qa_copied, 1)
                        attn_side(k % 16, lambda i, u=kk // 16: hd(u + i), g - 1)

            def merge(n, j, side):
                for k in range(N_GATE):
                    round_step(n, k)
                    if side and k < 2 * KT:
                        h0 = (GROUPS - 1) * GH + k // 16
                        attn_load(k % 16, lambda i: h0 + i, GROUPS - 1, ((GROUPS - 1) % 2) * 2, k // 16)
                        if k == 3:
                            silu(flat(((GROUPS - 1) % 2) * 2 + 1), 1, n(0))
                        attn_side(k % 16, lambda i: h0 + i, GROUPS - 1)
                    if k == KT + 3:
                        act.wait_ge(pe_done, n(KT))
                        nc.scalar.activation(flat(j), acc[:, 0, :], ACT.Sigmoid).then_inc(sig_a_done, 1)
                    if k == 2 * KT + 3:
                        act.wait_ge(pe_done, n(2 * KT))
                        nc.scalar.activation(sig_b[:, :, :], acc[:, 1, :].rearrange("p (h t) -> p h t", h=GH), ACT.Sigmoid).then_inc(sig_b_done, 1)

            merge(count(N_AT), 0, True)
            with act.Fori(1, NB) as j:
                merge(count(N_AT, N_GATE, j), j, False)

            def project(n, first, a):
                for b in range(2):
                    for k in range(KT):
                        if first and b == 0 and k in Y_AT:
                            j = Y_AT.index(k)
                            act.wait_ge(y_done, j + 1)
                            nc.scalar.activation(h_hi[:, j * GH:(j + 1) * GH, :], heads(j), ACT.Copy).then_inc(y_hi_done, 1)
                        round_step(n, b * KT + k)
                        if k == 6 and not (first and b == 0):
                            squares(a(b - 1))

            def squares(i):
                act.wait_ge(res_done, i + 1)
                for t in range(TT):
                    m = nc.scalar.activation(sq_o[:, :], xr[:, t, bass.ds(i * BLK, BLK)], ACT.Square,
                                             accum_out=ssq[:, t, bass.ds(i, 1)])
                    m.then_inc(rsq_done, 1)
                    act.wait_ge(rsq_done, i * 2 + (t + 1))

            project(count(N_MERGE), True, count(0))
            with act.Fori(1, NB // 2) as m:
                project(count(N_MERGE, 2 * KT, m), False, count(0, 2, m))
            squares(NB - 1)
            act.wait_ge(fs_sum, 1)
            nc.scalar.activation(small[:, 2:4], small[:, 0:2], ACT.Sqrt, scale=1.0 / D, bias=eps_t[:, :]).then_inc(fs_root, 1)
            act.wait_ge(fs_rs, 1)
            act.wait_ge(gained, NB)
            for i in range(4):
                cols = slice(i * (D // 4), (i + 1) * (D // 4))
                nc.scalar.activation(xr[:, 1, cols], xr[:, 1, cols], ACT.Copy, scale=small[:, 5:6]).then_inc(fin_s, 1)

        @block.vector
        def _(dve):
            def rest_step(n, k):
                dve.wait_ge(hi_ready, n(k + 1))
                nc.vector.tensor_tensor(w_lo[:, k % RING, :], raw[:, (k // 2) % RING, k % 2, :],
                                        w_hi[:, k % RING, :].bitcast(F32), ALU.subtract).then_inc(lo_ready, 1)

            def hgrn_side(k, hd, f_count, z_count, slot, b):
                if k == 0:
                    dve.wait_ge(sig_f_done, f_count)
                    dve.wait_ge(lb_ready, 2)
                    f = heads(slot)[:, b, :]
                    nc.vector.tensor_scalar(fg[:, :], f, oml[:, bass.ds(hd(0), 1)], lb[:, bass.ds(hd(0), 1)], ALU.mult, ALU.add).then_inc(fg_done, 1)
                    dve.wait_ge(fg_done, hd(1))
                    nc.vector.tensor_scalar(kf[:, :], fg[:, :], -1.0, 1.0, ALU.mult, ALU.add).then_inc(kf_done, 1)
                if k == 2:
                    dve.wait_ge(ln_done, hd(1))
                    nc.vector.tensor_tensor_scan(g_view, tab[:, T_SCAN:T_SCAN + SEQ], gl[:, :], 0.0, ALU.mult, ALU.add).then_inc(g_done, 1)
                if k in (3, 4, 5):
                    if k == 3:
                        dve.wait_ge(g_done, hd(1))
                    for i in (2 * (k - 3), 2 * (k - 3) + 1):
                        m = HALVES[i]
                        gv = g_view.rearrange("p (c two m) -> p c two m", two=2, m=m)
                        dv = decay[:, i, :].rearrange("p (c two m) -> p c two m", two=2, m=m)
                        mid = gv[:, :, 0, m - 1:m].broadcast_to([P, SEQ // (2 * m), m])
                        nc.vector.tensor_tensor(dv[:, :, 0, :], mid, gv[:, :, 0, :], ALU.subtract)
                        nc.vector.tensor_tensor(dv[:, :, 1, :], gv[:, :, 1, :], mid, ALU.subtract)
                    if k == 5:
                        gv = g_view.rearrange("p (c t) -> p c t", t=CHUNK)
                        end = gv[:, :, CHUNK - 1:CHUNK].broadcast_to([P, CHUNKS, CHUNK])
                        nc.vector.tensor_tensor(decay[:, L_END, :].rearrange("p (c t) -> p c t", t=CHUNK), end, gv,
                                                ALU.subtract).then_inc(dec_args, 1)
                if k in (8, 9, 10, 11):
                    qh = heads(slot + 1)[:, b, :]
                    if k in (8, 10):
                        dve.wait_ge(dec_done, hd(0) * 2 + (k - 6) // 2)
                    if k == 8:
                        dve.wait_ge(kf_done, hd(1))
                        dve.wait_ge(silu_done, z_count - 1)
                    for i in (() if k == 11 else (2 * (k - 8), 2 * (k - 8) + 1)):
                        m = HALVES[i]
                        dv = decay[:, i, :].rearrange("p (c two m) -> p c two m", two=2, m=m)
                        kv = kf[:, :].rearrange("p (c two m) -> p c two m", two=2, m=m)
                        qv = qh.rearrange("p (c two m) -> p c two m", two=2, m=m)
                        nc.vector.tensor_tensor(dv[:, :, 0, :], dv[:, :, 0, :], kv[:, :, 0, :], ALU.mult)
                        nc.vector.tensor_tensor(dv[:, :, 1, :], dv[:, :, 1, :], qv[:, :, 1, :], ALU.mult)
                    if k == 11:
                        nc.vector.tensor_tensor(qg[:, :], g_view, qh, ALU.mult)
                        nc.vector.tensor_tensor(decay[:, L_END, :], decay[:, L_END, :], kf[:, :], ALU.mult).then_inc(dec_mul, 1)
                if k in (15, 20):
                    t = (k - 15) // 5
                    dve.wait_ge(levels_done, hd(0) * 2 + (t + 1))
                    nc.vector.tensor_tensor(lev_m[:, :, :], lev[:, 0:(NL + 1) * P].rearrange("p (l t) -> p l t", t=P),
                                            tab[:, T_LEV:T_LEV + (NL + 1) * P].rearrange("p (l t) -> p l t", t=P),
                                            ALU.mult).then_inc(masked, 1)
                if k in (16, 21):
                    t = (k - 16) // 5
                    dve.wait_ge(masked, hd(0) * 2 + (t + 1))
                    nc.vector.tensor_reduce(at_m[:, t, :], lev_m[:, :, :].rearrange("p l t -> p t l"), AX_X, ALU.add).then_inc(att_done, 1)
                if k == 19:
                    dve.wait_ge(kv_done, hd(1))
                    nc.vector.tensor_copy(state[:, 0, :], kv_spot[0]).then_inc(st_done[0], 1)
                    for c in range(1, CHUNKS - 1):
                        dve.wait_ge(st_done[c - 1], hd(1))
                        end = g_view[:, c * CHUNK + CHUNK - 1:c * CHUNK + CHUNK]
                        nc.vector.scalar_tensor_tensor(state[:, c, :], state[:, c - 1, :], end, kv_spot[c],
                                                       ALU.mult, ALU.add).then_inc(st_done[c], 1)
                if k == 29:
                    dve.wait_ge(root_done, hd(1))
                    nc.vector.reciprocal(rs[:, :], rs[:, :]).then_inc(rs_done, 1)
                if k == 30:
                    dve.wait_ge(rs_done, hd(1))
                    nc.vector.scalar_tensor_tensor(bb1[:, :], outp[:, 0:SEQ], vec[:, bass.ds(hd(64), 1)], rs[:, :],
                                                   ALU.mult, ALU.mult).then_inc(bb1_done, 1)
                    dve.wait_ge(bb1_done, hd(1))
                    dve.wait_ge(silu_done, z_count)
                    nc.vector.tensor_tensor(bb2[:, :], bb1[:, :], heads(slot + 3)[:, b, :], ALU.mult).then_inc(bb2_done, 1)
                if k == 31:
                    dve.wait_ge(b_hi_done, hd(1))
                    hi = b_hi[:, bass.ds(hd(0), 1), :].rearrange("p one t -> p (one t)").bitcast(F32)
                    nc.vector.tensor_tensor(b_lo[:, bass.ds(hd(0), 1), :].rearrange("p one t -> p (one t)"), bb2[:, :], hi,
                                            ALU.subtract).then_inc(b_lo_done, 1)

            def attn_side(k, hd, z_count, zslot, b):
                cuts = (slice(0, P), slice(P, P + SEQ))
                if k == 4:
                    dve.wait_ge(score_done, hd(1))
                    nc.vector.tensor_tensor(s_sb[:, :], lev[:, 0:P + SEQ], tab[:, T_AM:T_AM + P + SEQ], ALU.add).then_inc(s_masked, 1)
                    dve.wait_ge(s_masked, hd(1))
                    nc.vector.reduce_max(mx[:, 0:1], s_sb[:, cuts[0]], AX_X)
                    nc.vector.reduce_max(mx[:, 1:2], s_sb[:, cuts[1]], AX_X).then_inc(mx_done, 1)
                    dve.wait_ge(mx_done, hd(1))
                    nc.vector.tensor_scalar(negm[:, 0:TT], mx[:, 0:TT], sink[:, bass.ds(hd(0), 1)], -1.0, ALU.max, ALU.mult
                                            ).then_inc(negm_done, 1)
                if k == 5:
                    dve.wait_ge(p_exp, hd(1))
                    nc.vector.tensor_tensor(den[:, 0:TT], rowsum[:, 0:TT], esink[:, 0:TT], ALU.add).then_inc(den_done, 1)
                    dve.wait_ge(den_done, hd(1))
                    nc.vector.reciprocal(rden[:, 0:TT], den[:, 0:TT]).then_inc(rden_done, 1)
                    dve.wait_ge(rden_done, hd(1))
                    nc.vector.tensor_scalar(s_sb[:, cuts[0]], s_sb[:, cuts[0]], rden[:, 0:1], None, ALU.mult)
                    nc.vector.tensor_scalar(s_sb[:, cuts[1]], s_sb[:, cuts[1]], rden[:, 1:2], None, ALU.mult).then_inc(p_norm, 1)
                if k == 13:
                    dve.wait_ge(pv_done, hd(1))
                    dve.wait_ge(silu_done, z_count)
                    nc.vector.tensor_tensor(aa[:, :], outp[:, 0:SEQ], heads(zslot)[:, b, :], ALU.mult).then_inc(aa_done, 1)
                if k == 14:
                    dve.wait_ge(a_hi_done, hd(1))
                    hi = a_hi[:, bass.ds(hd(0), 1), :].rearrange("p one t -> p (one t)").bitcast(F32)
                    nc.vector.tensor_tensor(a_lo[:, bass.ds(hd(0), 1), :].rearrange("p one t -> p (one t)"), aa[:, :], hi,
                                            ALU.subtract).then_inc(a_lo_done, 1)

            dve.wait_ge(sink_in, 16)
            dve.wait_ge(tab_in, 16)
            nc.vector.memset(eps_t[:, :], EPS).then_inc(eps_set, 1)
            dve.wait_ge(vec_tr, 1)
            nc.vector.tensor_copy(vec[:, :], outp[:, 0:80]).then_inc(vec_ready, 1)
            dve.wait_ge(xsq, 4)
            sums = small[:, 0:4].rearrange("p (t half) -> p t half", half=2)
            nc.vector.tensor_reduce(small[:, 4:6], sums, AX_X, ALU.add).then_inc(xs_sum, 1)
            dve.wait_ge(xs_root, 1)
            nc.vector.reciprocal(small[:, 8:10], small[:, 6:8]).then_inc(xs_rs, 1)
            dve.wait_ge(xs_rs, 1)

            def scale_input(i):
                cols = slice(i * (D // 4), (i + 1) * (D // 4))
                for t in range(TT):
                    nc.vector.tensor_scalar(x_in[:, t, cols], x_in[:, t, cols], small[:, 8 + t:9 + t], None, ALU.mult).then_inc(x_scaled, 1)

            def input_pair(p):
                dve.wait_ge(h_hi_done, p + 1)
                for i in range(2):
                    kt = 2 * p + i
                    m = nc.vector.scalar_tensor_tensor(h_lo[:, kt, :], spots[p % 4][:, i * SEQ:(i + 1) * SEQ], vec[:, kt:kt + 1],
                                                       h_hi[:, kt, :].bitcast(F32), ALU.mult, ALU.subtract)
                m.then_inc(h_lo_done, 1)

            scale_input(0)
            l0, l1 = vec[:, 32:48], vec[:, 48:64]
            dve.wait_ge(vec_ready, 1)
            nc.vector.tensor_tensor(lbw[:, 32:48], l0, l1, ALU.max).then_inc(lb_chain, 1)
            dve.wait_ge(lb_chain, 1)
            nc.vector.tensor_tensor(lbw[:, 0:16], l0, lbw[:, 32:48], ALU.subtract)
            nc.vector.tensor_tensor(lbw[:, 16:32], l1, lbw[:, 32:48], ALU.subtract).then_inc(lb_chain, 1)
            dve.wait_ge(lb_exp, 1)
            nc.vector.tensor_tensor(lbw[:, 48:64], lbw[:, 0:16], lbw[:, 16:32], ALU.add).then_inc(lb_chain, 1)
            dve.wait_ge(lb_chain, 3)
            nc.vector.reciprocal(lbw[:, 64:80], lbw[:, 48:64]).then_inc(lb_chain, 1)
            dve.wait_ge(lb_chain, 4)
            nc.vector.tensor_tensor(lb[:, :], lbw[:, 0:16], lbw[:, 64:80], ALU.mult).then_inc(lb_ready, 1)
            dve.wait_ge(lb_ready, 1)
            nc.vector.tensor_scalar(oml[:, :], lb[:, :], -1.0, 1.0, ALU.mult, ALU.add).then_inc(lb_ready, 1)
            scale_input(1)
            input_pair(0)

            def hgrn_group(n, hd, g, prev_slot, side):
                for b in range(4):
                    for k in range(KT):
                        if not side and b == 0 and k % 2 == 0 and k // 2 + 1 < KT // 2:
                            input_pair(k // 2 + 1)
                            if k in (2, 8):
                                scale_input(2 + (k - 2) // 6)
                        rest_step(n, b * KT + k)
                        if side:
                            hgrn_side(k, lambda i, b=b: hd(b + i), g, g * 2, prev_slot, b)

            hgrn_group(count(0), None, 0, 4, False)
            with dve.Fori(1, GROUPS) as g:
                hgrn_group(count(0, 4 * KT, g), count(-GH, GH, g), g, ((g + 1) % 2) * 4, True)

            last_set = ((GROUPS - 1) % 2) * 4
            n = count(N_HG)
            for b in range(4):
                for k in range(KT):
                    rest_step(n, b * KT + k)
                    hgrn_side(k, lambda i, b=b: (GROUPS - 1) * GH + b + i, GROUPS, 2 * GROUPS, last_set, b)

            with dve.Fori(1, GROUPS) as g:
                n = count(N_KV, 2 * KT, g)
                hd = count(-GH, GH, g)
                for b in range(2):
                    for k in range(KT):
                        kk = b * KT + k
                        rest_step(n, kk)
                        attn_side(k % 16, lambda i, u=kk // 16: hd(u + i), g + 2 * GROUPS, ((g + 1) % 2) * 2 + 1, kk // 16)

            def merge(n, j, side):
                for k in range(N_GATE):
                    rest_step(n, k)
                    if side and k < 2 * KT:
                        zs = ((GROUPS - 1) % 2) * 2 + 1
                        attn_side(k % 16, lambda i: (GROUPS - 1) * GH + k // 16 + i, 3 * GROUPS, zs, k // 16)
                    if k == 3 and not side:
                        add_b(j - 1, n(0))
                    if k == 2 * KT + UT + 3:
                        dve.wait_ge(pe_done, n(2 * KT + UT))
                        dve.wait_ge(sig_a_done, j + 1)
                        nc.vector.tensor_tensor(flat(j), flat(j), acc[:, 0, :], ALU.mult).then_inc(ya_done, 1)

            def add_b(j, n_end):
                dve.wait_ge(pe_done, n_end)
                dve.wait_ge(sig_b_done, j + 1)
                sb_flat = sig_b[:, :, :].rearrange("p h t -> p (h t)")
                nc.vector.tensor_tensor(sb_flat, sb_flat, acc[:, 1, :], ALU.mult).then_inc(yb_part, 1)
                dve.wait_ge(yb_part, j + 1)
                dve.wait_ge(ya_done, j + 1)
                nc.vector.tensor_tensor(flat(j), flat(j), sb_flat, ALU.add).then_inc(y_done, 1)

            merge(count(N_AT), 0, True)
            with dve.Fori(1, NB) as j:
                merge(count(N_AT, N_GATE, j), j, False)

            def residual(i, par, n_end):
                dve.wait_ge(pe_done, n_end)
                cols = bass.ds(i * BLK, BLK)
                nc.vector.tensor_tensor(xr[:, :, cols], xr[:, :, cols], acc[:, par, :].rearrange("p (t n) -> p t n", t=TT), ALU.add
                                        ).then_inc(res_done, 1)

            def apply_gain(i):
                dve.wait_ge(rsq_done, i * 2 + 2)
                cols = bass.ds(i * BLK, BLK)
                gv = fgain[:, cols].unsqueeze(1).broadcast_to([P, TT, BLK])
                nc.vector.tensor_tensor(xr[:, :, cols], xr[:, :, cols], gv, ALU.mult).then_inc(gained, 1)

            def project(n, first, a):
                for b in range(2):
                    for k in range(KT):
                        if first and b == 0 and k in Y_AT:
                            j = Y_AT.index(k)
                            dve.wait_ge(y_hi_done, j + 1)
                            nc.vector.tensor_tensor(h_lo[:, j * GH:(j + 1) * GH, :], heads(j),
                                                    h_hi[:, j * GH:(j + 1) * GH, :].bitcast(F32), ALU.subtract).then_inc(y_lo_done, 1)
                        rest_step(n, b * KT + k)
                        if first and b == 0 and k == 3:
                            add_b(NB - 1, N_MERGE)
                        if not (first and b == 0):
                            if k == 3:
                                dve.wait_ge(xr_in[(b - 1) % 2], (a(b - 1, 2) + 1) * 32)
                                residual(a(b - 1), (b - 1) % 2, n(b * KT))
                            if k == 9:
                                apply_gain(a(b - 1))

            project(count(N_MERGE), True, count(0))
            with dve.Fori(1, NB // 2) as m:
                project(count(N_MERGE, 2 * KT, m), False, count(0, 2, m))
            dve.wait_ge(xr_in[1], (NB // 2) * 32)
            residual(NB - 1, 1, N_MERGE + NB * KT)
            dve.wait_ge(rsq_done, 2 * NB)
            nc.vector.tensor_reduce(small[:, 0:2], ssq[:, :, :], AX_X, ALU.add).then_inc(fs_sum, 1)
            apply_gain(NB - 1)
            dve.wait_ge(fs_root, 1)
            nc.vector.reciprocal(small[:, 4:6], small[:, 2:4]).then_inc(fs_rs, 1)
            dve.wait_ge(gained, NB)
            dve.wait_ge(fs_rs, 1)
            for i in range(4):
                cols = slice(i * (D // 4), (i + 1) * (D // 4))
                nc.vector.tensor_scalar(xr[:, 0, cols], xr[:, 0, cols], small[:, 4:5], None, ALU.mult).then_inc(fin_v, 1)


_INS = ["x", "norm_gain", "w_in", "attn_sinks", "lb_logits", "hgrn_norm_gain", "w_up_attn", "w_up_hgrn",
        "w_out", "final_norm_gain"]


def constant_tables(np):
    tab = np.zeros((P, T_ALL), np.float32)
    i = np.arange(P)
    s, t = i[:, None], i[None, :]
    for n, m in enumerate(HALVES):
        own = (s // (2 * m) == t // (2 * m)) & (s % (2 * m) < m) & (t % (2 * m) >= m)
        tab[:, T_LEV + n * P:T_LEV + (n + 1) * P] = own
    tab[:, T_LEV + NL * P:T_LEV + (NL + 1) * P] = s == t
    for tile in range(TT):
        first = T_AM + tile * P
        width = P * (tile + 1)
        tc = (tile * P + i[:, None]) // CHUNK
        sc = np.arange(width)[None, :] // CHUNK
        tab[:, first:first + width] = np.where((sc == tc) | (sc == tc - 1), 0.0, -3e38)
    tab[:, T_SCAN:T_SCAN + SEQ] = np.arange(SEQ) % CHUNK != 0
    tab[:, T_ID:T_ID + P] = s == t
    tab[:, T_MEAN:T_MEAN + P] = 1.0 / HD
    return tab


def kernel(**inputs):
    import numpy as _np
    import concourse.bacc as _bacc
    from concourse import mybir as _mybir
    from concourse.bass_utils import run_bass_kernel_spmd as _run

    nc = _bacc.Bacc("TRN2", target_bir_lowering=False, num_devices=1)
    arrays, args = {}, []
    for name in _INS:
        a = _np.ascontiguousarray(inputs[name])
        arrays[f"in_{name}_dram"] = a
        args.append(nc.dram_tensor(f"in_{name}_dram", a.shape, _mybir.dt.from_np(a.dtype), kind="ExternalInput").ap())
    arrays["tables_dram"] = constant_tables(_np)
    args.append(nc.dram_tensor("tables_dram", (P, T_ALL), _mybir.dt.float32, kind="ExternalInput").ap())
    args.append(nc.dram_tensor("out_0_dram", (1, SEQ, D), _mybir.dt.float32, kind="ExternalOutput").ap())
    build(nc, *args)
    r = _run(nc, [arrays], core_ids=[0])
    return r.results[0]["out_0_dram"]
```

```python
from contextlib import ExitStack

import concourse.bass as bass
from concourse import mybir

P = 128
F32 = mybir.dt.float32
F32R = mybir.dt.float32r
ALU = mybir.AluOpType
ACT = mybir.ActivationFunctionType
AX = mybir.AxisListType
AX_X = AX.X

SEQ = 256
TT = SEQ // P
D = 4096
KT = D // P
HD = 128
HEADS = 16
KVH = 4
GH = 4
GROUPS = HEADS // GH
CHUNK = 64
CHUNKS = SEQ // CHUNK
BLK = GH * HD
WID = HEADS * HD
UT = WID // P
NB = D // BLK
EPS = 1e-6
SCALE = float(HD) ** -0.5

C_QA, C_KA, C_VA, C_ZA = 0, WID, WID + KVH * HD, WID + 2 * KVH * HD
C_QB = C_ZA + WID
C_FB, C_IB, C_ZB = C_QB + WID, C_QB + 2 * WID, C_QB + 3 * WID
C_GA = C_ZB + WID
C_GB = C_GA + D

HALVES = [P // 2 >> i for i in range(7)]
NL = len(HALVES)
INNER = range(1, NL - 1)
L_G = len(INNER)
L_END = L_G + 1
L_X = L_END + 1
SEEN = P + CHUNK
NEAR = P + P // 2

T_LEV = 0
T_DIAG = T_LEV + NL * P // 2
T_AM = T_DIAG + P
T_SCAN = T_AM + P + SEEN
T_ID = T_SCAN + SEQ
T_MEAN = T_ID + P
T_ALL = T_MEAN + P

X_PIECES = [(0, 0, D // 2, D // 2), (0, D // 2, D, 3 * D // 4),
            (1, 0, D // 2, D // 2), (1, D // 2, 3 * D // 4, 3 * D // 4), (1, 3 * D // 4, D, 7 * D // 8)]
FINAL = [0, BLK] + [D - BLK - i * 2 * BLK for i in (2, 1, 0)] + [D]

RING = 4

N_HG = GROUPS * 4 * KT
N_KV = N_HG + 2 * KT
N_AT = N_KV + GROUPS * 2 * KT
N_GATE = 2 * KT + 2 * UT
N_MERGE = N_AT + NB * N_GATE


Y_AT = [0, 2] + [GH * (j - 1) for j in range(2, NB)]


def count(base, per=0, it=0):
    def c(k=0, unit=1):
        if isinstance(it, int):
            return (base + per * it + k) // unit
        assert per % unit == 0
        return it * (per // unit) + (base + k) // unit
    return c


def build(nc, x, norm_gain, w_in, attn_sinks, lb_logits, hgrn_norm_gain, w_up_attn, w_up_hgrn,
          w_out, final_norm_gain, tables, out):
    ctx = ExitStack()
    with ctx:
        def sb(name, shape, dt=F32):
            return ctx.enter_context(nc.sbuf_tensor(name, shape, dt))

        def sem(name):
            return ctx.enter_context(nc.semaphore(name))

        raw = sb("raw", [P, RING, 2, BLK])
        w_hi = sb("w_hi", [P, RING, BLK], F32R)
        w_lo = sb("w_lo", [P, RING, BLK], F32R)
        h_hi = sb("h_hi", [P, KT, SEQ], F32R)
        h_lo = sb("h_lo", [P, KT, SEQ], F32R)
        region_base = nc.sbuf_base
        sb("branch_region", [P, 4 * UT * SEQ])
        proj_base = nc.sbuf_base
        sb("proj_region", [P, NB * GH * SEQ])
        k_att = sb("k_att", [P, GH, SEQ])
        v_att = sb("v_att", [P, TT, BLK])
        tab = sb("tab", [P, T_ALL])
        vec = sb("vec", [P, 80])
        lb = sb("lb", [P, HEADS])
        oml = sb("oml", [P, HEADS])
        sink = sb("sink", [P, HEADS])
        ssq = sb("ssq", [P, TT, NB])
        small = sb("small", [P, 16])
        sums = sb("sums", [P, 2 * len(X_PIECES)])
        eps_t = sb("eps_t", [P, 1])

        def at(base, name, shape, dt=F32):
            n = 4
            for s in shape[1:]:
                n *= s
            return nc.alloc_sbuf_tensor_at(name, shape, dt, offset=base), base + n

        a_hi, b1 = at(region_base, "a_hi", [P, UT, SEQ], F32R)
        a_lo, b2 = at(b1, "a_lo", [P, UT, SEQ], F32R)
        b_hi, b3 = at(b2, "b_hi", [P, UT, SEQ], F32R)
        b_lo, _ = at(b3, "b_lo", [P, UT, SEQ], F32R)
        decay, q = at(region_base, "decay", [P, L_X + 1, SEQ])
        lev_m, q = at(q, "lev_m", [P, NL + 1, P])
        at_m, q = at(q, "at_m", [P, TT, P])
        fg, q = at(q, "fg", [P, SEQ])
        kf, q = at(q, "kf", [P, SEQ])
        gl, q = at(q, "gl", [P, SEQ])
        qn, q = at(q, "qn", [P, TT, NEAR])
        cross, q = at(q, "cross", [P, P])
        iv, q = at(q, "iv", [P, TT, HD])
        osq, q = at(q, "osq", [P, SEQ])
        rs, q = at(q, "rs", [P, SEQ])
        bb1, q = at(q, "bb1", [P, SEQ])
        bb2, q = at(q, "bb2", [P, SEQ])
        assert q <= b2
        x_in, q = at(region_base, "x_in", [P, TT, D])
        vrow, q = at(q, "vrow", [80, P])
        lbw, q = at(q, "lbw", [P, 80])
        xr, q = at(region_base, "xr", [P, TT, D])
        fgain, q = at(q, "fgain", [P, D])
        sq_o, q = at(q, "sq_o", [P, BLK])
        proj, _ = at(proj_base, "proj", [P, NB, GH * SEQ])
        sq_x, q = at(proj_base, "sq_x", [P, D // 2])
        sq_v, q = at(q, "sq_v", [P, D // 4])
        q = proj_base + 4 * 4 * GH * SEQ
        s_sb, q = at(q, "s_sb", [P, P + SEQ])
        p_t, q = at(q, "p_t", [P, 3, P])
        qw, q = at(q, "qw", [P, SEQ])
        vw, q = at(q, "vw", [P, TT, HD])
        aa, q = at(q, "aa", [P, SEQ])
        mx, q = at(q, "mx", [P, 8])
        negm, q = at(q, "negm", [P, 8])
        rowsum, q = at(q, "rowsum", [P, 8])
        esink, q = at(q, "esink", [P, 8])
        den, q = at(q, "den", [P, 8])
        rden, q = at(q, "rden", [P, 8])
        sig_b = k_att

        acc = ctx.enter_context(nc.psum_tensor("acc", [P, 2, 2 * BLK], F32))
        lev = ctx.enter_context(nc.psum_tensor("lev", [P, 2 * 512], F32))
        mis = ctx.enter_context(nc.psum_tensor("mis", [P, 512], F32))
        outp = ctx.enter_context(nc.psum_tensor("outp", [P, 512], F32))

        w_landed = [sem(f"w_landed{i}") for i in range(RING)]
        hi_ready = sem("hi_ready")
        lo_ready = sem("lo_ready")
        pe_done = sem("pe_done")
        tile0_done = sem("tile0_done")
        ident_in, tab_in, vec_in, sink_in = sem("ident_in"), sem("tab_in"), sem("vec_in"), sem("sink_in")
        x_landed = [sem(f"x_landed{i}") for i in range(len(X_PIECES))]
        eps_set = sem("eps_set")
        xsq, xsq_v, sums_zero = sem("xsq"), sem("xsq_v"), sem("sums_zero")
        xs_sum, xs_root, xs_rs, x_scaled, x_scaled_1 = sem("xs_sum"), sem("xs_root"), sem("xs_rs"), sem("x_scaled"), sem("x_scaled_1")
        x_tr, h_hi_done, h_lo_done = sem("x_tr"), sem("h_hi_done"), sem("h_lo_done")
        vec_tr, vec_ready = sem("vec_tr"), sem("vec_ready")
        lb_chain, lb_exp, lb_ready = sem("lb_chain"), sem("lb_exp"), sem("lb_ready")
        sig_f_done = sem("sig_f_done")
        silu_done, i_copied, kv_copied, qa_copied = sem("silu_done"), sem("i_copied"), sem("kv_copied"), sem("qa_copied")
        fg_done, kf_done, ln_done, g_done = sem("fg_done"), sem("kf_done"), sem("ln_done"), sem("g_done")
        dec_args, dec_done, dec_mul, iv_done = sem("dec_args"), sem("dec_done"), sem("dec_mul"), sem("iv_done")
        levels_done, cross_done, cross_copied = sem("levels_done"), sem("cross_done"), sem("cross_copied")
        ends_used, masked, att_done = sem("ends_used"), sem("masked"), sem("att_done")
        ho_done, osq_done, mean_done, root_done, rs_done = sem("ho_done"), sem("osq_done"), sem("mean_done"), sem("root_done"), sem("rs_done")
        bb1_done, bb2_done, b_hi_done, b_lo_done = sem("bb1_done"), sem("bb2_done"), sem("b_hi_done"), sem("b_lo_done")
        qvw_done, score_done, s_masked, mx_done, negm_done = sem("qvw_done"), sem("score_done"), sem("s_masked"), sem("mx_done"), sem("negm_done")
        unseen_zero = sem("unseen_zero")
        p_exp, den_done, rden_done, p_norm = sem("p_exp"), sem("den_done"), sem("rden_done"), sem("p_norm")
        p_tr, pt_copied, pv_done, aa_done, a_hi_done, a_lo_done = sem("p_tr"), sem("pt_copied"), sem("pv_done"), sem("aa_done"), sem("a_hi_done"), sem("a_lo_done")
        sig_a_done, sig_b_done, ya_done, yb_part, y_done = sem("sig_a_done"), sem("sig_b_done"), sem("ya_done"), sem("yb_part"), sem("y_done")
        y_hi_done, y_lo_done = sem("y_hi_done"), sem("y_lo_done")
        xr_in = [sem("xr_in0"), sem("xr_in1")]
        res_done, rsq_done, gained = sem("res_done"), sem("rsq_done"), sem("gained")
        fs_sum, fs_root, fs_rs, stored = sem("fs_sum"), sem("fs_root"), sem("fs_rs"), sem("stored")
        fin_0, fin_1 = sem("fin_0"), sem("fin_1")

        ident = tab[:, T_ID:T_ID + P]
        x_rows = x.rearrange("b (t p) d -> p (b t) d", p=P)
        out_rows = out.rearrange("b (t p) d -> p (b t) d", p=P)
        w_in_r = w_in.rearrange("l (c p) n -> p (l c) n", p=P)
        w_ua_r = w_up_attn.rearrange("l (c p) n -> p (l c) n", p=P)
        w_uh_r = w_up_hgrn.rearrange("l (c p) n -> p (l c) n", p=P)
        w_out_r = w_out.rearrange("l (c p) n -> p (l c) n", p=P)
        g_view = decay[:, L_G, :]

        def level_scores(t, i):
            half = P // 2
            if i == 0:
                o = mis[:, t * half:(t + 1) * half]
            elif i in INNER:
                o = lev[:, t * 512 + (i - 1) * half:t * 512 + i * half]
            else:
                o = near_scores(t)[:, P:NEAR]
            return o.rearrange("p (c m) -> p c m", m=HALVES[i])

        def late_half(ap, i):
            return ap.rearrange("p (c two m) -> p c two m", two=2, m=HALVES[i])[:, :, 1, :]

        def near_scores(t):
            return lev[:, (t + 1) * 512 - NEAR:(t + 1) * 512]

        spots = [lev[:, 0:512], lev[:, 512:1024], mis[:, :], outp[:, :]]

        def heads(slot):
            return proj[:, bass.ds(slot, 1), :].rearrange("p one (h t) -> p (one h) t", h=GH)

        def flat(slot):
            return proj[:, bass.ds(slot, 1), :].rearrange("p one n -> p (one n)")

        def rows(slot):
            return proj[:, bass.ds(slot, 1), :].rearrange("p one (t n) -> p (one t) n", t=TT)

        block = ctx.enter_context(nc.Block())

        @block.sync
        def _(sp):
            for i, (t, first, end, _) in enumerate(X_PIECES):
                sp.dma_start(x_in[:, t, first:end], x_rows[:, t, first:end]).then_inc(x_landed[i], 16)
                if i == 1:
                    sp.dma_start(vrow[0:32, :], norm_gain.rearrange("a (c p) -> (a c) p", p=P)).then_inc(vec_in, 16)
                    sp.dma_start(vrow[32:64, :], lb_logits.rearrange("a (c p) -> (a c) p", p=P)).then_inc(vec_in, 16)
                    sp.dma_start(vrow[64:80, :], hgrn_norm_gain.rearrange("a (c p) -> (a c) p", p=P)).then_inc(vec_in, 16)
                    sp.dma_start(sink[:, :], attn_sinks.broadcast_to([P, HEADS])).then_inc(sink_in, 16)
                    sp.dma_start(tab[:, T_ID:], tables[:, T_ID:]).then_inc(ident_in, 16)

            def load_steps(n, w, col, steps, first=0):
                with sp.Fori(0, steps // (2 * RING)) as c:
                    for r in range(RING):
                        sp.wait_ge(lo_ready, c * (2 * RING) + n(2 * r - 2 * RING + 2))
                        sp.dma_start(raw[:, r, :, :], w[:, bass.ds(c * (2 * RING) + (first + 2 * r), 2), bass.ds(col, BLK)]
                                     ).then_inc(w_landed[r], 16)

            def load_first(w, col):
                for r in range(RING):
                    sp.dma_start(raw[:, r, :, :], w[:, 2 * r:2 * r + 2, bass.ds(col, BLK)]).then_inc(w_landed[r], 16)
                sp.dma_start(tab[:, 0:T_ID], tables[:, 0:T_ID]).then_inc(tab_in, 16)
                with sp.Fori(1, KT // (2 * RING)) as c:
                    for r in range(RING):
                        sp.wait_ge(lo_ready, c * (2 * RING) + (2 * r - 2 * RING + 2))
                        sp.dma_start(raw[:, r, :, :], w[:, bass.ds(c * (2 * RING) + 2 * r, 2), bass.ds(col, BLK)]
                                     ).then_inc(w_landed[r], 16)

            load_first(w_in_r, C_FB)
            for b, c0 in ((1, C_QB), (2, C_IB), (3, C_ZB)):
                load_steps(count(b * KT), w_in_r, c0, KT)
            with sp.Fori(1, GROUPS) as g:
                for b, c0 in enumerate((C_FB, C_QB, C_IB, C_ZB)):
                    load_steps(count(b * KT, 4 * KT, g), w_in_r, g * BLK + c0, KT)
            load_steps(count(N_HG), w_in_r, C_KA, KT)
            load_steps(count(N_HG + KT), w_in_r, C_VA, KT)
            with sp.Fori(0, GROUPS) as g:
                for b, c0 in enumerate((C_QA, C_ZA)):
                    load_steps(count(N_KV + b * KT, 2 * KT, g), w_in_r, g * BLK + c0, KT)
            with sp.Fori(0, NB) as j:
                load_steps(count(N_AT, N_GATE, j), w_in_r, j * BLK + C_GA, KT)
                load_steps(count(N_AT + KT, N_GATE, j), w_in_r, j * BLK + C_GB, KT)
                load_steps(count(N_AT + 2 * KT, N_GATE, j), w_ua_r, j * BLK, UT)
                load_steps(count(N_AT + 2 * KT + UT, N_GATE, j), w_uh_r, j * BLK, UT)
            fgain_rows = final_norm_gain.rearrange("(a d) -> a d", a=1).broadcast_to([P, D])

            def load_tail(n, par):
                cols = bass.ds(n * BLK, BLK)
                sp.dma_start(xr[:, :, cols], x_rows[:, :, cols]).then_inc(xr_in[par], 16)
                sp.dma_start(fgain[:, cols], fgain_rows[:, cols]).then_inc(xr_in[par], 16)

            load_steps(count(N_MERGE), w_out_r, 0, KT // 2)
            sp.wait_ge(pe_done, N_MERGE)
            load_tail(0, 0)
            load_steps(count(N_MERGE + KT // 2), w_out_r, 0, KT // 2, first=KT // 2)
            load_tail(1, 1)
            load_steps(count(N_MERGE + KT), w_out_r, BLK, KT)
            with sp.Fori(1, NB // 2) as m:
                for b in range(2):
                    load_tail(m * 2 + b, b)
                    load_steps(count(N_MERGE + b * KT, 2 * KT, m), w_out_r, m * (2 * BLK) + b * BLK, KT)
            for i in range(len(FINAL) - 1):
                cols = slice(FINAL[i], FINAL[i + 1])
                for t, fin in enumerate((fin_0, fin_1)):
                    sp.wait_ge(fin, i + 1)
                    sp.dma_start(out_rows[:, t, cols], xr[:, t, cols]).then_inc(stored, 16)
            sp.wait_ge(stored, (len(FINAL) - 1) * TT * 16)

        @block.tensor
        def _(pe):
            def step_t(n, k, par, r_hi, r_lo, kt, last, free):
                s = k % RING
                if kt == 0 and free is not None:
                    pe.wait_ge(*free)
                pe.wait_ge(lo_ready, n(k + 1))
                for c in range(GH):
                    o = acc[:, par, c * SEQ:(c + 1) * SEQ]
                    cols = slice(c * HD, (c + 1) * HD)
                    first = kt == 0 and c % 2 == 0
                    nc.tensor.matmul(o, w_hi[:, s, cols], r_hi[:, kt, :], start=first, stop=False)
                    nc.tensor.matmul(o, w_hi[:, s, cols], r_lo[:, kt, :], start=False, stop=False)
                    m = nc.tensor.matmul(o, w_lo[:, s, cols], r_hi[:, kt, :], start=False, stop=last and c % 2 == 1)
                m.then_inc(pe_done, 1)

            def step_r(n, k, par, kt, last, free, rows_done=None):
                s = k % RING
                if kt == 0 and free is not None:
                    pe.wait_ge(*free)
                pe.wait_ge(lo_ready, n(k + 1))
                for t in range(TT):
                    o = acc[:, par, t * BLK:(t + 1) * BLK]
                    tok = slice(t * P, (t + 1) * P)
                    nc.tensor.matmul(o, h_hi[:, kt, tok], w_hi[:, s, :], start=kt == 0, stop=False)
                    nc.tensor.matmul(o, h_lo[:, kt, tok], w_hi[:, s, :], start=False, stop=False)
                    m = nc.tensor.matmul(o, h_hi[:, kt, tok], w_lo[:, s, :], start=False, stop=last)
                    if last and t == 0 and rows_done is not None:
                        m.then_inc(rows_done, 1)
                m.then_inc(pe_done, 1)

            def levels(t):
                tok = slice(t * P, (t + 1) * P)
                for i in INNER:
                    nc.tensor.matmul(level_scores(t, i), decay[:, i - 1, tok], late_half(decay[:, i - 1, tok], i),
                                     start=True, stop=True)
                nc.tensor.matmul(near_scores(t), kf[:, tok], qn[:, t, :], start=True, stop=True).then_inc(levels_done, 1)

            def hgrn_side(k, hd):
                if k == 14:
                    pe.wait_ge(dec_mul, hd(1))
                    nc.tensor.matmul(outp[:, SEQ:SEQ + P], decay[:, L_X, 0:P], decay[:, L_X, P:SEQ],
                                     start=True, stop=True).then_inc(cross_done, 1)
                    for t in range(TT):
                        nc.tensor.matmul(level_scores(t, 0), decay[:, L_END, t * P:(t + 1) * P],
                                         late_half(decay[:, L_G, t * P:(t + 1) * P], 0), start=True, stop=True)
                    levels(0)
                if k == 18:
                    levels(1)
                if k == 22:
                    pe.wait_ge(iv_done, hd(1))
                    pe.wait_ge(cross_copied, hd(1))
                    pe.wait_ge(att_done, hd(0) * 2 + 2)
                    nc.tensor.matmul(outp[:, 0:P], iv[:, 0, :], at_m[:, 0, :], start=True, stop=True)
                    nc.tensor.matmul(outp[:, P:SEQ], iv[:, 1, :], at_m[:, 1, :], start=True, stop=False)
                    m = nc.tensor.matmul(outp[:, P:SEQ], iv[:, 0, :], cross[:, :], start=False, stop=True)
                    m.then_inc(ho_done, 1)
                if k == 24:
                    pe.wait_ge(osq_done, hd(1))
                    nc.tensor.matmul(mis[:, 0:SEQ], tab[:, T_MEAN:T_MEAN + P], osq[:, :],
                                     start=True, stop=True).then_inc(mean_done, 1)

            def attn_side(k, hd, g):
                if k == 1:
                    pe.wait_ge(qvw_done, hd(1))
                    keys = k_att[:, bass.ds(g, 1), :].rearrange("p one t -> p (one t)")
                    nc.tensor.matmul(lev[:, 0:P], qw[:, 0:P], keys[:, 0:P], start=True, stop=True)
                    nc.tensor.matmul(lev[:, P:P + SEEN], qw[:, P:SEQ], keys[:, SEQ - SEEN:], start=True, stop=True).then_inc(score_done, 1)
                if k == 8:
                    pe.wait_ge(unseen_zero, 1)
                    pe.wait_ge(p_norm, hd(1))
                    for i in range(3):
                        m = nc.tensor.transpose(mis[:, i * P:(i + 1) * P], s_sb[:, i * P:(i + 1) * P], ident)
                    m.then_inc(p_tr, 1)
                if k == 11:
                    pe.wait_ge(pt_copied, hd(1))
                    nc.tensor.matmul(outp[:, 0:P], vw[:, 0, :], p_t[:, 0, :], start=True, stop=True)
                    nc.tensor.matmul(outp[:, P:SEQ], vw[:, 0, :], p_t[:, 1, :], start=True, stop=False)
                    nc.tensor.matmul(outp[:, P:SEQ], vw[:, 1, :], p_t[:, 2, :], start=False, stop=True).then_inc(pv_done, 1)

            pe.wait_ge(vec_in, 48)
            pe.wait_ge(ident_in, 16)
            nc.tensor.transpose(outp[:, 0:80], vrow[0:80, :], ident[0:80, 0:80]).then_inc(vec_tr, 1)
            def input_pair(p):
                pe.wait_ge(x_scaled, p + 1)
                if p < 3:
                    pe.wait_ge(x_scaled_1, p + 1)
                if p == 3:
                    pe.wait_ge(vec_ready, 1)
                if p >= 4:
                    pe.wait_ge(h_lo_done, p - 3)
                for i in range(2):
                    for t in range(TT):
                        kt = 2 * p + i
                        m = nc.tensor.transpose(spots[p % 4][:, (i * TT + t) * P:(i * TT + t + 1) * P],
                                                x_in[:, t, kt * P:(kt + 1) * P], ident)
                m.then_inc(x_tr, 1)

            def hgrn_group(n, g, hd, side):
                before = [(i_copied, g), (silu_done, g * 2), (sig_f_done, g + 1), (silu_done, g * 2 + 1)]
                for b in range(4):
                    free = before[b] if side or b >= 2 else None
                    for k in range(KT):
                        kk = b * KT + k
                        if not side and b == 0 and k % 2 == 0:
                            pe.wait_ge(h_lo_done, k // 2 + 1)
                        if b == 2:
                            step_r(n, kk, b % 2, k, k == KT - 1, free)
                        else:
                            step_t(n, kk, b % 2, h_hi, h_lo, k, k == KT - 1, free)
                        if side:
                            hgrn_side(k, lambda i, b=b: hd(b + i))
                        elif b == 0 and k % 2 == 0 and k // 2 + 3 < KT // 2:
                            input_pair(k // 2 + 3)

            for p in range(3):
                input_pair(p)
            hgrn_group(count(0), 0, None, False)
            with pe.Fori(1, GROUPS) as g:
                hgrn_group(count(0, 4 * KT, g), g, count(-GH, GH, g), True)

            last_set = ((GROUPS - 1) % 2) * 4
            n = count(N_HG)
            before = [(i_copied, GROUPS), (silu_done, 2 * GROUPS), (kv_copied, 1), (kv_copied, 2)]
            for b in range(4):
                for k in range(KT):
                    kk = b * KT + k
                    free = before[b]
                    if b == 1:
                        step_r(n, kk, b % 2, k, k == KT - 1, free)
                    else:
                        step_t(n, kk, b % 2, h_hi, h_lo, k, k == KT - 1, free)
                    hgrn_side(k, lambda i, b=b: (GROUPS - 1) * GH + b + i)

            def attn_blocks(n, hd, g):
                before = [(qa_copied, g + 1), (silu_done, g + (2 * GROUPS + 1))]
                for b in range(2):
                    for k in range(KT):
                        kk = b * KT + k
                        step_t(n, kk, b % 2, h_hi, h_lo, k, k == KT - 1, before[b])
                        attn_side(k % 16, lambda i, u=kk // 16: hd(u + i), g)

            with pe.Fori(1, GROUPS) as g:
                attn_blocks(count(N_KV, 2 * KT, g), count(-GH, GH, g), g - 1)

            def merge(n, j, side):
                before = [(qa_copied, GROUPS), (silu_done, 3 * GROUPS)] if side else [(ya_done, j), (yb_part, j)]
                for k in range(2 * KT):
                    step_t(n, k, k // KT, h_hi, h_lo, k % KT, k % KT == KT - 1, before[k // KT])
                    if side:
                        attn_side(k % 16, lambda i, u=k // 16: (GROUPS - 1) * GH + u + i, GROUPS - 1)
                if side:
                    pe.wait_ge(a_lo_done, HEADS)
                    pe.wait_ge(b_lo_done, HEADS)
                for k in range(UT):
                    step_t(n, 2 * KT + k, 0, a_hi, a_lo, k, k == UT - 1, (sig_a_done, j + 1))
                for k in range(UT):
                    step_t(n, 2 * KT + UT + k, 1, b_hi, b_lo, k, k == UT - 1, (sig_b_done, j + 1))

            merge(count(N_AT), 0, True)
            with pe.Fori(1, NB) as j:
                merge(count(N_AT, N_GATE, j), j, False)

            def project(n, before, first):
                for b in range(2):
                    for k in range(KT):
                        if first and b == 0 and k % GH == 0:
                            pe.wait_ge(y_lo_done, k // GH + 1)
                        step_r(n, b * KT + k, b, k, k == KT - 1, before[b], tile0_done)

            project(count(N_MERGE), [(ya_done, NB), (yb_part, NB)], True)
            with pe.Fori(1, NB // 2) as m:
                project(count(N_MERGE, 2 * KT, m), [(res_done, m * 4 - 2), (res_done, m * 4)], False)

        @block.scalar
        def _(act):
            def round_step(n, k, fresh=False):
                if k % 2 == 0:
                    act.wait_ge(w_landed[(k // 2) % RING], (n(k, 2 * RING) + 1) * 16)
                if not (fresh and k < RING):
                    act.wait_ge(pe_done, n(k - RING + 1))
                nc.scalar.activation(w_hi[:, k % RING, :], raw[:, (k // 2) % RING, k % 2, :], ACT.Copy).then_inc(hi_ready, 1)

            def silu(dst, par, n_end):
                act.wait_ge(pe_done, n_end)
                nc.scalar.activation(dst, acc[:, par, :], ACT.Silu).then_inc(silu_done, 1)

            def hgrn_epilogue(b, par, n_end, slot):
                if b == 2:
                    act.wait_ge(pe_done, n_end)
                    nc.scalar.activation(flat(slot + 2), acc[:, par, :], ACT.Copy).then_inc(i_copied, 1)
                elif b == 0:
                    act.wait_ge(pe_done, n_end)
                    nc.scalar.activation(flat(slot), acc[:, par, :], ACT.Sigmoid).then_inc(sig_f_done, 1)
                else:
                    silu(flat(slot + b), par, n_end)

            def hgrn_side(k, hd, groups, slot, b):
                if k == 11:
                    if b == 0:
                        act.wait_ge(i_copied, groups)
                    nc.scalar.activation(iv[:, :, :], rows(slot + 2)[:, :, b * HD:(b + 1) * HD], ACT.Copy).then_inc(iv_done, 1)
                if k == 2:
                    act.wait_ge(fg_done, hd(1))
                    nc.scalar.activation(gl[:, :], fg[:, :], ACT.Ln).then_inc(ln_done, 1)
                if k in (7, 9):
                    act.wait_ge(dec_args, hd(1))
                    part = decay[:, 0:4, :] if k == 7 else decay[:, 4:L_END + 1, :]
                    nc.scalar.activation(part, part, ACT.Exp).then_inc(dec_done, 1)
                if k == 16:
                    act.wait_ge(cross_done, hd(1))
                    nc.scalar.activation(cross[:, :], outp[:, SEQ:SEQ + P], ACT.Copy).then_inc(cross_copied, 1)
                if k == 24:
                    act.wait_ge(ho_done, hd(1))
                    nc.scalar.activation(osq[:, :], outp[:, 0:SEQ], ACT.Square).then_inc(osq_done, 1)
                if k == 26:
                    act.wait_ge(mean_done, hd(1))
                    nc.scalar.activation(rs[:, :], mis[:, 0:SEQ], ACT.Sqrt, bias=eps_t[:, :]).then_inc(root_done, 1)
                if k == 31:
                    act.wait_ge(bb2_done, hd(1))
                    nc.scalar.activation(b_hi[:, bass.ds(hd(0), 1), :].rearrange("p one t -> p (one t)"), bb2[:, :], ACT.Copy
                                         ).then_inc(b_hi_done, 1)

            def attn_side(k, hd):
                if k == 5:
                    act.wait_ge(negm_done, hd(1))
                    cuts = (slice(0, P), slice(P + SEQ - SEEN, P + SEQ))
                    for t in range(TT):
                        nc.scalar.activation(s_sb[:, cuts[t]], s_sb[:, cuts[t]], ACT.Exp, bias=negm[:, t:t + 1],
                                             accum_out=rowsum[:, t:t + 1])
                    nc.scalar.activation(esink[:, 0:TT], negm[:, 0:TT], ACT.Exp, bias=sink[:, bass.ds(hd(0), 1)]).then_inc(p_exp, 1)
                if k == 10:
                    act.wait_ge(p_tr, hd(1))
                    nc.scalar.activation(p_t[:, :, :], mis[:, 0:3 * P].rearrange("p (i t) -> p i t", i=3), ACT.Copy).then_inc(pt_copied, 1)
                if k == 14:
                    act.wait_ge(aa_done, hd(1))
                    nc.scalar.activation(a_hi[:, bass.ds(hd(0), 1), :].rearrange("p one t -> p (one t)"), aa[:, :], ACT.Copy
                                         ).then_inc(a_hi_done, 1)

            def attn_load(k, g, qslot, b):
                if k == 0:
                    act.wait_ge(qa_copied, g + 1)
                    act.wait_ge(kv_copied, 2)
                    nc.scalar.activation(qw[:, :], heads(qslot)[:, b, :], ACT.Copy, scale=SCALE)
                    nc.scalar.activation(vw[:, :, :], v_att[:, :, bass.ds(g * HD, HD)], ACT.Copy).then_inc(qvw_done, 1)

            act.wait_ge(sink_in, 16)
            act.wait_ge(eps_set, 1)
            nc.scalar.activation(small[:, 0:1], eps_t[:, :], ACT.Sqrt)
            for i, (t, first, end, cut) in enumerate(X_PIECES):
                act.wait_ge(x_landed[i], 16)
                if i:
                    act.wait_ge(xsq, i)
                nc.scalar.activation(sq_x[:, 0:cut - first], x_in[:, t, first:cut], ACT.Square, accum_out=sums[:, i:i + 1]
                                     ).then_inc(xsq, 1)
            act.wait_ge(xs_sum, TT)
            nc.scalar.activation(small[:, 6:8], small[:, 4:6], ACT.Sqrt, scale=1.0 / D, bias=eps_t[:, :]).then_inc(xs_root, 1)
            act.wait_ge(xs_rs, 1)
            for p in range(3):
                cols = slice(2 * p * P, 2 * (p + 1) * P)
                nc.scalar.activation(x_in[:, 1, cols], x_in[:, 1, cols], ACT.Copy, scale=small[:, 9:10]).then_inc(x_scaled_1, 1)
            act.wait_ge(vec_ready, 1)

            def input_pair(p):
                act.wait_ge(x_tr, p + 1)
                for i in range(2):
                    kt = 2 * p + i
                    m = nc.scalar.activation(h_hi[:, kt, :], spots[p % 4][:, i * SEQ:(i + 1) * SEQ], ACT.Copy, scale=vec[:, kt:kt + 1])
                m.then_inc(h_hi_done, 1)
            round_step(count(0), 0, fresh=True)
            round_step(count(0), 1, fresh=True)
            input_pair(0)

            def hgrn_group(n, hd, g, slot, prev_slot, side, first=False):
                for b in range(4):
                    for k in range(KT):
                        kk = b * KT + k
                        if first and b == 0 and k % 2 == 0 and k // 2 + 1 < KT // 2:
                            input_pair(k // 2 + 1)
                        if first and b == 0:
                            if k + 2 < KT:
                                round_step(n, k + 2, fresh=True)
                        else:
                            round_step(n, kk)
                        if first and b == 1 and k == 4:
                            act.wait_ge(lb_chain, 2)
                            nc.scalar.activation(lbw[:, 0:32], lbw[:, 0:32], ACT.Exp).then_inc(lb_exp, 1)
                        if k == 12 and not (first and b == 0):
                            pb = (b - 1) % 4
                            hgrn_epilogue(pb, pb % 2, n(b * KT), slot if b else prev_slot)
                        if side:
                            hgrn_side(k, lambda i, b=b: hd(b + i), g, prev_slot, b)

            hgrn_group(count(0), None, 0, 0, 4, False, first=True)
            with act.Fori(1, GROUPS) as g:
                hgrn_group(count(0, 4 * KT, g), count(-GH, GH, g), g, (g % 2) * 4, ((g + 1) % 2) * 4, True)

            last_set = ((GROUPS - 1) % 2) * 4
            n = count(N_HG)
            for b in range(4):
                for k in range(KT):
                    round_step(n, b * KT + k)
                    if k == 12:
                        if b == 0:
                            hgrn_epilogue(3, 1, n(0), last_set)
                        elif b == 1:
                            act.wait_ge(pe_done, n(KT))
                            nc.scalar.activation(k_att[:, :, :], acc[:, 0, :].rearrange("p (h t) -> p h t", h=GH), ACT.Copy).then_inc(kv_copied, 1)
                        elif b == 2:
                            act.wait_ge(pe_done, n(2 * KT))
                            nc.scalar.activation(v_att[:, :, :], acc[:, 1, :].rearrange("p (t c) -> p t c", t=TT), ACT.Copy).then_inc(kv_copied, 1)
                        else:
                            act.wait_ge(pe_done, n(3 * KT))
                            nc.scalar.activation(flat(0), acc[:, 0, :], ACT.Copy).then_inc(qa_copied, 1)
                    hgrn_side(k, lambda i, b=b: (GROUPS - 1) * GH + b + i, GROUPS, last_set, b)

            with act.Fori(1, GROUPS) as g:
                n = count(N_KV, 2 * KT, g)
                hd = count(-GH, GH, g)
                for b in range(2):
                    for k in range(KT):
                        kk = b * KT + k
                        round_step(n, kk)
                        attn_load(k % 16, g - 1, ((g + 1) % 2) * 2, kk // 16)
                        if k == 7 and b == 0:
                            silu(flat(((g + 1) % 2) * 2 + 1), 1, n(0))
                        if k == 7 and b == 1:
                            act.wait_ge(pe_done, n(KT))
                            nc.scalar.activation(flat((g % 2) * 2), acc[:, 0, :], ACT.Copy).then_inc(qa_copied, 1)
                        attn_side(k % 16, lambda i, u=kk // 16: hd(u + i))

            def merge(n, j, side):
                for k in range(N_GATE):
                    round_step(n, k)
                    if side and k < 2 * KT:
                        h0 = (GROUPS - 1) * GH + k // 16
                        attn_load(k % 16, GROUPS - 1, ((GROUPS - 1) % 2) * 2, k // 16)
                        if k == 7:
                            silu(flat(((GROUPS - 1) % 2) * 2 + 1), 1, n(0))
                        attn_side(k % 16, lambda i: h0 + i)
                    if k == KT + 8:
                        act.wait_ge(pe_done, n(KT))
                        nc.scalar.activation(flat(j), acc[:, 0, :], ACT.Sigmoid).then_inc(sig_a_done, 1)
                    if k == 2 * KT + 3:
                        act.wait_ge(pe_done, n(2 * KT))
                        nc.scalar.activation(sig_b[:, :, :], acc[:, 1, :].rearrange("p (h t) -> p h t", h=GH), ACT.Sigmoid).then_inc(sig_b_done, 1)

            merge(count(N_AT), 0, True)
            with act.Fori(1, NB) as j:
                merge(count(N_AT, N_GATE, j), j, False)

            def project(n, first, a):
                for b in range(2):
                    for k in range(KT):
                        if first and b == 0 and k in Y_AT:
                            j = Y_AT.index(k)
                            act.wait_ge(y_done, j + 1)
                            nc.scalar.activation(h_hi[:, j * GH:(j + 1) * GH, :], heads(j), ACT.Copy).then_inc(y_hi_done, 1)
                        round_step(n, b * KT + k)
                        if k == 6 and not (first and b == 0):
                            squares(a(b - 1))

            def squares(i):
                for t in range(TT):
                    act.wait_ge(res_done, i * 2 + (t + 1))
                    m = nc.scalar.activation(sq_o[:, :], xr[:, t, bass.ds(i * BLK, BLK)], ACT.Square,
                                             accum_out=ssq[:, t, bass.ds(i, 1)])
                    m.then_inc(rsq_done, 1)
                    act.wait_ge(rsq_done, i * 2 + (t + 1))

            project(count(N_MERGE), True, count(0))
            with act.Fori(1, NB // 2) as m:
                project(count(N_MERGE, 2 * KT, m), False, count(0, 2, m))
            nc.scalar.activation(small[:, 6:7], eps_t[:, :], ACT.Sqrt)
            squares(NB - 1)
            act.wait_ge(fs_sum, 1)
            nc.scalar.activation(small[:, 2:4], small[:, 0:2], ACT.Sqrt, scale=1.0 / D, bias=eps_t[:, :]).then_inc(fs_root, 1)
            act.wait_ge(fs_rs, 1)
            act.wait_ge(gained, NB - 1)
            for i in range(len(FINAL) - 2):
                cols = slice(FINAL[i], FINAL[i + 1])
                nc.scalar.activation(xr[:, 1, cols], xr[:, 1, cols], ACT.Copy, scale=small[:, 5:6]).then_inc(fin_1, 1)

        @block.vector
        def _(dve):
            def rest_step(n, k):
                dve.wait_ge(hi_ready, n(k + 1))
                nc.vector.tensor_tensor(w_lo[:, k % RING, :], raw[:, (k // 2) % RING, k % 2, :],
                                        w_hi[:, k % RING, :].bitcast(F32), ALU.subtract).then_inc(lo_ready, 1)

            def hgrn_side(k, hd, f_count, z_count, slot, b):
                if k == 0:
                    dve.wait_ge(sig_f_done, f_count)
                    dve.wait_ge(lb_ready, 2)
                    f = heads(slot)[:, b, :]
                    nc.vector.tensor_scalar(fg[:, :], f, oml[:, bass.ds(hd(0), 1)], lb[:, bass.ds(hd(0), 1)], ALU.mult, ALU.add).then_inc(fg_done, 1)
                    dve.wait_ge(fg_done, hd(1))
                    nc.vector.tensor_scalar(kf[:, :], fg[:, :], -1.0, 1.0, ALU.mult, ALU.add).then_inc(kf_done, 1)
                if k == 3:
                    dve.wait_ge(ln_done, hd(1))
                    nc.vector.tensor_tensor_scan(g_view, tab[:, T_SCAN:T_SCAN + SEQ], gl[:, :], 0.0, ALU.mult, ALU.add).then_inc(g_done, 1)
                if k in (4, 5, 6):
                    if k == 4:
                        dve.wait_ge(g_done, hd(1))
                    for i in {4: (1, 2), 5: (3, 4), 6: (5,)}[k]:
                        m = HALVES[i]
                        gv = g_view.rearrange("p (c two m) -> p c two m", two=2, m=m)
                        dv = decay[:, i - 1, :].rearrange("p (c two m) -> p c two m", two=2, m=m)
                        mid = gv[:, :, 0, m - 1:m].broadcast_to([P, SEQ // (2 * m), m])
                        nc.vector.tensor_tensor(dv[:, :, 0, :], mid, gv[:, :, 0, :], ALU.subtract)
                        nc.vector.tensor_tensor(dv[:, :, 1, :], gv[:, :, 1, :], mid, ALU.subtract)
                    if k == 6:
                        gv = g_view.rearrange("p (c t) -> p c t", t=CHUNK)
                        end = gv[:, :, CHUNK - 1:CHUNK].broadcast_to([P, CHUNKS, CHUNK])
                        nc.vector.tensor_tensor(decay[:, L_END, :].rearrange("p (c t) -> p c t", t=CHUNK), end, gv,
                                                ALU.subtract).then_inc(dec_args, 1)
                if k in (10, 11, 12, 13):
                    qh = heads(slot + 1)[:, b, :]
                    if k in (10, 12):
                        dve.wait_ge(dec_done, hd(0) * 2 + (k - 8) // 2)
                    if k == 10:
                        dve.wait_ge(kf_done, hd(1))
                        dve.wait_ge(silu_done, z_count - 1)
                    for i in {10: (1, 2), 11: (3, 4), 12: (5,), 13: ()}[k]:
                        m = HALVES[i]
                        dv = decay[:, i - 1, :].rearrange("p (c two m) -> p c two m", two=2, m=m)
                        kv = kf[:, :].rearrange("p (c two m) -> p c two m", two=2, m=m)
                        qv = qh.rearrange("p (c two m) -> p c two m", two=2, m=m)
                        nc.vector.tensor_tensor(dv[:, :, 0, :], dv[:, :, 0, :], kv[:, :, 0, :], ALU.mult)
                        nc.vector.tensor_tensor(dv[:, :, 1, :], dv[:, :, 1, :], qv[:, :, 1, :], ALU.mult)
                    if k == 12:
                        c0, c1, c2, c3 = (slice(c * CHUNK, (c + 1) * CHUNK) for c in range(CHUNKS))
                        nc.vector.scalar_tensor_tensor(decay[:, L_X, c0], decay[:, L_END, c0], g_view[:, 2 * CHUNK - 1:2 * CHUNK],
                                                       kf[:, c0], ALU.mult, ALU.mult)
                        nc.vector.tensor_tensor(decay[:, L_X, c1], decay[:, L_END, c1], kf[:, c1], ALU.mult)
                        nc.vector.tensor_tensor(decay[:, L_X, c2], g_view[:, c2], qh[:, c2], ALU.mult)
                        nc.vector.scalar_tensor_tensor(decay[:, L_X, c3], g_view[:, c3], g_view[:, 3 * CHUNK - 1:3 * CHUNK],
                                                       qh[:, c3], ALU.mult, ALU.mult).then_inc(ends_used, 1)
                        nc.vector.tensor_copy(qn[:, :, 0:P], qh.rearrange("p (t n) -> p t n", t=TT))
                    if k == 13:
                        odd = [v.rearrange("p (t c two) -> p t c two", t=TT, two=2)[:, :, :, 1] for v in (qh, fg[:, :])]
                        nc.vector.tensor_tensor(qn[:, :, P:NEAR], odd[0], odd[1], ALU.mult)
                        dve.wait_ge(ends_used, hd(1))
                        nc.vector.tensor_tensor(late_half(g_view, 0), late_half(g_view, 0), late_half(qh, 0), ALU.mult)
                        nc.vector.tensor_tensor(decay[:, L_END, :], decay[:, L_END, :], kf[:, :], ALU.mult).then_inc(dec_mul, 1)
                if k in (16, 20):
                    t = (k - 16) // 4
                    dve.wait_ge(levels_done, hd(0) * 2 + (t + 1))
                    for i in range(NL):
                        own = tab[:, T_LEV + i * P // 2:T_LEV + (i + 1) * P // 2].rearrange("p (c m) -> p c m", m=HALVES[i])
                        nc.vector.tensor_tensor(late_half(lev_m[:, i, :], i), level_scores(t, i), own, ALU.mult)
                    nc.vector.tensor_tensor(lev_m[:, NL, :], near_scores(t)[:, 0:P], tab[:, T_DIAG:T_DIAG + P],
                                            ALU.mult).then_inc(masked, 1)
                if k in (17, 21):
                    t = (k - 17) // 4
                    dve.wait_ge(masked, hd(0) * 2 + (t + 1))
                    nc.vector.tensor_reduce(at_m[:, t, :], lev_m[:, :, :].rearrange("p l t -> p t l"), AX_X, ALU.add).then_inc(att_done, 1)
                if k == 25:
                    dve.wait_ge(osq_done, hd(1))
                    dve.wait_ge(silu_done, z_count)
                    nc.vector.scalar_tensor_tensor(bb1[:, :], outp[:, 0:SEQ], vec[:, bass.ds(hd(64), 1)], heads(slot + 3)[:, b, :],
                                                   ALU.mult, ALU.mult).then_inc(bb1_done, 1)
                if k in (27, 28):
                    dve.wait_ge(root_done, hd(1))
                    tok = slice((k - 27) * P, (k - 26) * P)
                    nc.vector.reciprocal(rs[:, tok], rs[:, tok]).then_inc(rs_done, 1)
                if k == 29:
                    dve.wait_ge(rs_done, hd(0) * 2 + 2)
                    dve.wait_ge(bb1_done, hd(1))
                    nc.vector.tensor_tensor(bb2[:, :], bb1[:, :], rs[:, :], ALU.mult).then_inc(bb2_done, 1)
                if k == 31:
                    dve.wait_ge(b_hi_done, hd(1))
                    hi = b_hi[:, bass.ds(hd(0), 1), :].rearrange("p one t -> p (one t)").bitcast(F32)
                    nc.vector.tensor_tensor(b_lo[:, bass.ds(hd(0), 1), :].rearrange("p one t -> p (one t)"), bb2[:, :], hi,
                                            ALU.subtract).then_inc(b_lo_done, 1)

            def attn_side(k, hd, z_count, zslot, b):
                cuts = (slice(0, P), slice(P + SEQ - SEEN, P + SEQ))
                if k == 3:
                    dve.wait_ge(score_done, hd(1))
                    nc.vector.tensor_tensor(s_sb[:, cuts[0]], lev[:, 0:P], tab[:, T_AM:T_AM + P], ALU.add)
                    nc.vector.tensor_tensor(s_sb[:, cuts[1]], lev[:, P:P + SEEN], tab[:, T_AM + P:T_AM + P + SEEN], ALU.add
                                            ).then_inc(s_masked, 1)
                if k == 4:
                    dve.wait_ge(s_masked, hd(1))
                    nc.vector.reduce_max(mx[:, 0:1], s_sb[:, cuts[0]], AX_X)
                    nc.vector.reduce_max(mx[:, 1:2], s_sb[:, cuts[1]], AX_X).then_inc(mx_done, 1)
                    dve.wait_ge(mx_done, hd(1))
                    nc.vector.tensor_scalar(negm[:, 0:TT], mx[:, 0:TT], sink[:, bass.ds(hd(0), 1)], -1.0, ALU.max, ALU.mult
                                            ).then_inc(negm_done, 1)
                if k == 6:
                    dve.wait_ge(p_exp, hd(1))
                    nc.vector.tensor_tensor(den[:, 0:TT], rowsum[:, 0:TT], esink[:, 0:TT], ALU.add).then_inc(den_done, 1)
                    dve.wait_ge(den_done, hd(1))
                    nc.vector.reciprocal(rden[:, 0:TT], den[:, 0:TT]).then_inc(rden_done, 1)
                if k == 7:
                    dve.wait_ge(rden_done, hd(1))
                    nc.vector.tensor_scalar(s_sb[:, cuts[0]], s_sb[:, cuts[0]], rden[:, 0:1], None, ALU.mult)
                    nc.vector.tensor_scalar(s_sb[:, cuts[1]], s_sb[:, cuts[1]], rden[:, 1:2], None, ALU.mult).then_inc(p_norm, 1)
                if k == 13:
                    dve.wait_ge(pv_done, hd(1))
                    dve.wait_ge(silu_done, z_count)
                    nc.vector.tensor_tensor(aa[:, :], outp[:, 0:SEQ], heads(zslot)[:, b, :], ALU.mult).then_inc(aa_done, 1)
                if k == 15:
                    dve.wait_ge(a_hi_done, hd(1))
                    hi = a_hi[:, bass.ds(hd(0), 1), :].rearrange("p one t -> p (one t)").bitcast(F32)
                    nc.vector.tensor_tensor(a_lo[:, bass.ds(hd(0), 1), :].rearrange("p one t -> p (one t)"), aa[:, :], hi,
                                            ALU.subtract).then_inc(a_lo_done, 1)

            nc.vector.memset(eps_t[:, :], EPS).then_inc(eps_set, 1)
            dve.wait_ge(vec_tr, 1)
            nc.vector.tensor_copy(vec[:, :], outp[:, 0:80]).then_inc(vec_ready, 1)
            nc.vector.memset(sums[:, len(X_PIECES):], 0.0).then_inc(sums_zero, 1)
            done = 0
            for i, (t, _, end, cut) in enumerate(X_PIECES):
                if cut == end:
                    continue
                dve.wait_ge(x_landed[i], 16)
                if done == 0:
                    dve.wait_ge(sums_zero, 1)
                else:
                    dve.wait_ge(xsq_v, done)
                part = x_in[:, t, cut:end]
                nc.vector.scalar_tensor_tensor(sq_v[:, 0:end - cut], part, 1.0, part, ALU.mult, ALU.mult,
                                               accum_out=sums[:, len(X_PIECES) + i:len(X_PIECES) + i + 1]).then_inc(xsq_v, 1)
                done += 1
            dve.wait_ge(xsq, len(X_PIECES))
            dve.wait_ge(xsq_v, done)
            for t in range(TT):
                own = [i for i, piece in enumerate(X_PIECES) if piece[0] == t]
                halves = sums[:, :].rearrange("p (half i) -> p half i", half=2)[:, :, own[0]:own[-1] + 1]
                nc.vector.tensor_reduce(small[:, 4 + t:5 + t], halves, AX.XY, ALU.add).then_inc(xs_sum, 1)
            dve.wait_ge(xs_root, 1)
            nc.vector.reciprocal(small[:, 8:10], small[:, 6:8]).then_inc(xs_rs, 1)
            dve.wait_ge(xs_rs, 1)

            def scale_pair(p):
                cols = slice(2 * p * P, 2 * (p + 1) * P)
                for t in range(1 if p < 3 else TT):
                    m = nc.vector.tensor_scalar(x_in[:, t, cols], x_in[:, t, cols], small[:, 8 + t:9 + t], None, ALU.mult)
                m.then_inc(x_scaled, 1)

            def input_pair(p):
                dve.wait_ge(h_hi_done, p + 1)
                for i in range(2):
                    kt = 2 * p + i
                    m = nc.vector.scalar_tensor_tensor(h_lo[:, kt, :], spots[p % 4][:, i * SEQ:(i + 1) * SEQ], vec[:, kt:kt + 1],
                                                       h_hi[:, kt, :].bitcast(F32), ALU.mult, ALU.subtract)
                m.then_inc(h_lo_done, 1)

            for p in range(3):
                scale_pair(p)
            rest_step(count(0), 0)
            rest_step(count(0), 1)
            dve.wait_ge(vec_ready, 1)
            input_pair(0)

            def lower_bound(k):
                if k == 1:
                    dve.wait_ge(sink_in, 16)
                    dve.wait_ge(tab_in, 16)
                    l0, l1 = vec[:, 32:48], vec[:, 48:64]
                    nc.vector.tensor_tensor(lbw[:, 32:48], l0, l1, ALU.max).then_inc(lb_chain, 1)
                    dve.wait_ge(lb_chain, 1)
                    nc.vector.tensor_tensor(lbw[:, 0:16], l0, lbw[:, 32:48], ALU.subtract)
                    nc.vector.tensor_tensor(lbw[:, 16:32], l1, lbw[:, 32:48], ALU.subtract).then_inc(lb_chain, 1)
                if k == 8:
                    dve.wait_ge(lb_exp, 1)
                    nc.vector.tensor_tensor(lbw[:, 48:64], lbw[:, 0:16], lbw[:, 16:32], ALU.add).then_inc(lb_chain, 1)
                    dve.wait_ge(lb_chain, 3)
                    nc.vector.reciprocal(lbw[:, 64:80], lbw[:, 48:64]).then_inc(lb_chain, 1)
                    dve.wait_ge(lb_chain, 4)
                    nc.vector.tensor_tensor(lb[:, :], lbw[:, 0:16], lbw[:, 64:80], ALU.mult).then_inc(lb_ready, 1)
                    dve.wait_ge(lb_ready, 1)
                    nc.vector.tensor_scalar(oml[:, :], lb[:, :], -1.0, 1.0, ALU.mult, ALU.add).then_inc(lb_ready, 1)

            def hgrn_group(n, hd, g, prev_slot, side):
                for b in range(4):
                    for k in range(KT):
                        if not side and b == 0 and k % 2 == 0 and k // 2 + 1 < KT // 2:
                            if k // 2 + 3 < KT // 2:
                                scale_pair(k // 2 + 3)
                            input_pair(k // 2 + 1)
                        if not side and b == 0:
                            if k + 2 < KT:
                                rest_step(n, k + 2)
                        else:
                            rest_step(n, b * KT + k)
                        if not side and b == 1:
                            lower_bound(k)
                        if not side and b == 1 and k == 0:
                            dve.wait_ge(h_lo_done, KT // 2)
                            nc.vector.memset(lev_m[:, :, :], 0.0)
                        if side:
                            hgrn_side(k, lambda i, b=b: hd(b + i), g, g * 2, prev_slot, b)

            hgrn_group(count(0), None, 0, 4, False)
            with dve.Fori(1, GROUPS) as g:
                hgrn_group(count(0, 4 * KT, g), count(-GH, GH, g), g, ((g + 1) % 2) * 4, True)

            last_set = ((GROUPS - 1) % 2) * 4
            n = count(N_HG)
            for b in range(4):
                for k in range(KT):
                    rest_step(n, b * KT + k)
                    hgrn_side(k, lambda i, b=b: (GROUPS - 1) * GH + b + i, GROUPS, 2 * GROUPS, last_set, b)

            nc.vector.memset(s_sb[:, P:P + SEQ - SEEN], 0.0).then_inc(unseen_zero, 1)
            with dve.Fori(1, GROUPS) as g:
                n = count(N_KV, 2 * KT, g)
                hd = count(-GH, GH, g)
                for b in range(2):
                    for k in range(KT):
                        kk = b * KT + k
                        rest_step(n, kk)
                        attn_side(k % 16, lambda i, u=kk // 16: hd(u + i), g + 2 * GROUPS, ((g + 1) % 2) * 2 + 1, kk // 16)

            def merge(n, j, side):
                for k in range(N_GATE):
                    rest_step(n, k)
                    if side and k < 2 * KT:
                        zs = ((GROUPS - 1) % 2) * 2 + 1
                        attn_side(k % 16, lambda i: (GROUPS - 1) * GH + k // 16 + i, 3 * GROUPS, zs, k // 16)
                    if k == 3 and not side:
                        add_b(j - 1, n(0))
                    if k == 2 * KT + UT + 3:
                        dve.wait_ge(pe_done, n(2 * KT + UT))
                        dve.wait_ge(sig_a_done, j + 1)
                        nc.vector.tensor_tensor(flat(j), flat(j), acc[:, 0, :], ALU.mult).then_inc(ya_done, 1)

            def add_b(j, n_end):
                dve.wait_ge(pe_done, n_end)
                dve.wait_ge(sig_b_done, j + 1)
                sb_flat = sig_b[:, :, :].rearrange("p h t -> p (h t)")
                nc.vector.tensor_tensor(sb_flat, sb_flat, acc[:, 1, :], ALU.mult).then_inc(yb_part, 1)
                dve.wait_ge(yb_part, j + 1)
                dve.wait_ge(ya_done, j + 1)
                nc.vector.tensor_tensor(flat(j), flat(j), sb_flat, ALU.add).then_inc(y_done, 1)

            merge(count(N_AT), 0, True)
            with dve.Fori(1, NB) as j:
                merge(count(N_AT, N_GATE, j), j, False)

            def residual(i, par, n_end):
                cols = bass.ds(i * BLK, BLK)
                for t in range(TT):
                    if t == 0:
                        dve.wait_ge(tile0_done, i + 1)
                    else:
                        dve.wait_ge(pe_done, n_end)
                    nc.vector.tensor_tensor(xr[:, t, cols], xr[:, t, cols], acc[:, par, t * BLK:(t + 1) * BLK], ALU.add
                                            ).then_inc(res_done, 1)

            def apply_gain(i):
                dve.wait_ge(rsq_done, i * 2 + 2)
                cols = bass.ds(i * BLK, BLK)
                gv = fgain[:, cols].unsqueeze(1).broadcast_to([P, TT, BLK])
                nc.vector.tensor_tensor(xr[:, :, cols], xr[:, :, cols], gv, ALU.mult).then_inc(gained, 1)

            def project(n, first, a):
                for b in range(2):
                    for k in range(KT):
                        if first and b == 0 and k in Y_AT:
                            j = Y_AT.index(k)
                            dve.wait_ge(y_hi_done, j + 1)
                            nc.vector.tensor_tensor(h_lo[:, j * GH:(j + 1) * GH, :], heads(j),
                                                    h_hi[:, j * GH:(j + 1) * GH, :].bitcast(F32), ALU.subtract).then_inc(y_lo_done, 1)
                        rest_step(n, b * KT + k)
                        if first and b == 0 and k == 3:
                            add_b(NB - 1, N_MERGE)
                        if not (first and b == 0):
                            if k == 3:
                                dve.wait_ge(xr_in[(b - 1) % 2], (a(b - 1, 2) + 1) * 32)
                                residual(a(b - 1), (b - 1) % 2, n(b * KT))
                            if k == 9:
                                apply_gain(a(b - 1))

            project(count(N_MERGE), True, count(0))
            with dve.Fori(1, NB // 2) as m:
                project(count(N_MERGE, 2 * KT, m), False, count(0, 2, m))
            dve.wait_ge(xr_in[1], (NB // 2) * 32)
            residual(NB - 1, 1, N_MERGE + NB * KT)
            dve.wait_ge(rsq_done, 2 * NB)
            nc.vector.tensor_reduce(small[:, 0:2], ssq[:, :, :], AX_X, ALU.add).then_inc(fs_sum, 1)
            dve.wait_ge(fs_root, 1)
            nc.vector.reciprocal(small[:, 4:6], small[:, 2:4]).then_inc(fs_rs, 1)
            dve.wait_ge(gained, NB - 1)
            dve.wait_ge(fs_rs, 1)
            for i in range(len(FINAL) - 2):
                cols = slice(FINAL[i], FINAL[i + 1])
                nc.vector.tensor_scalar(xr[:, 0, cols], xr[:, 0, cols], small[:, 4:5], None, ALU.mult).then_inc(fin_0, 1)
            last = slice(D - BLK, D)
            for t, fin in enumerate((fin_0, fin_1)):
                if t == 1:
                    dve.wait_ge(fin_1, len(FINAL) - 2)
                nc.vector.scalar_tensor_tensor(xr[:, t, last], xr[:, t, last], small[:, 4 + t:5 + t], fgain[:, last],
                                               ALU.mult, ALU.mult).then_inc(fin, 1)


_INS = ["x", "norm_gain", "w_in", "attn_sinks", "lb_logits", "hgrn_norm_gain", "w_up_attn", "w_up_hgrn",
        "w_out", "final_norm_gain"]


def constant_tables(np):
    tab = np.zeros((P, T_ALL), np.float32)
    i = np.arange(P)
    s, t = i[:, None], i[None, :]
    for n, m in enumerate(HALVES):
        own = (s // (2 * m) == t // (2 * m)) & (s % (2 * m) < m)
        tab[:, T_LEV + n * P // 2:T_LEV + (n + 1) * P // 2] = own[:, i % (2 * m) >= m]
    tab[:, T_DIAG:T_DIAG + P] = s == t
    for tile in range(TT):
        first = T_AM + tile * P
        keys = np.arange(P) if tile == 0 else np.arange(SEQ - SEEN, SEQ)
        tc = (tile * P + i[:, None]) // CHUNK
        sc = keys[None, :] // CHUNK
        tab[:, first:first + len(keys)] = np.where((sc == tc) | (sc == tc - 1), 0.0, -3e38)
    tab[:, T_SCAN:T_SCAN + SEQ] = np.arange(SEQ) % CHUNK != 0
    tab[:, T_ID:T_ID + P] = s == t
    tab[:, T_MEAN:T_MEAN + P] = 1.0 / HD
    return tab


def kernel(**inputs):
    import numpy as _np
    import concourse.bacc as _bacc
    from concourse import mybir as _mybir
    from concourse.bass_utils import run_bass_kernel_spmd as _run

    nc = _bacc.Bacc("TRN2", target_bir_lowering=False, num_devices=1)
    arrays, args = {}, []
    for name in _INS:
        a = _np.ascontiguousarray(inputs[name])
        arrays[f"in_{name}_dram"] = a
        args.append(nc.dram_tensor(f"in_{name}_dram", a.shape, _mybir.dt.from_np(a.dtype), kind="ExternalInput").ap())
    arrays["tables_dram"] = constant_tables(_np)
    args.append(nc.dram_tensor("tables_dram", (P, T_ALL), _mybir.dt.float32, kind="ExternalInput").ap())
    args.append(nc.dram_tensor("out_0_dram", (1, SEQ, D), _mybir.dt.float32, kind="ExternalOutput").ap())
    build(nc, *args)
    r = _run(nc, [arrays], core_ids=[0])
    return r.results[0]["out_0_dram"]
```
